# Optimizing a Trainium2 kernel written in Bass

```python
import jax, jax.numpy as jnp
from jax import lax
import numpy as np
import math

D_MODEL = 1024
BATCH = 1
SEQ = 512
DEPTH = 2

N_A_LAYERS = DEPTH // 2
N_B_LAYERS = DEPTH - N_A_LAYERS
HGRN_EXPAND = 128
HGRN_HEADS = D_MODEL // HGRN_EXPAND
HGRN_DK = HGRN_EXPAND
HGRN_DV = D_MODEL // HGRN_HEADS
HGRN_CHUNK = 64
MLA_HEADS = 16
MLA_NOPE = 128
MLA_ROPE = 64
MLA_V = 128
MLA_Q_LORA = 256
MLA_KV_LORA = 256
ROPE_THETA = 10000.0
QBLOCK = 128
D_FF = 4 * D_MODEL
EPS = 1e-6


def rmsnorm(x, gain):
    xf = x.astype(jnp.float32)
    y = xf * lax.rsqrt(jnp.mean(xf * xf, axis=-1, keepdims=True) + EPS)
    return (y * gain.astype(jnp.float32)).astype(x.dtype)

def rope_tables(seq):
    half = MLA_ROPE // 2
    inv_freq = ROPE_THETA ** (-jnp.arange(half, dtype=jnp.float32) / half)
    ang = jnp.arange(seq, dtype=jnp.float32)[:, None] * inv_freq[None, :]
    return jnp.cos(ang), jnp.sin(ang)

def apply_rope(x, cos, sin):
    half = MLA_ROPE // 2
    xf = x.astype(jnp.float32)
    x1, x2 = xf[..., :half], xf[..., half:]
    return jnp.concatenate([x1 * cos - x2 * sin, x2 * cos + x1 * sin], axis=-1).astype(x.dtype)

def hgrn_lower_bounds(lb_logits):
    return jnp.cumsum(jax.nn.softmax(lb_logits.astype(jnp.float32), axis=0), axis=0)

def hgrn2_mixer(xn, w_q, w_f, w_i, w_g, g_norm, w_o, lb):
    bsz, seq, _ = xn.shape
    nc = seq // HGRN_CHUNK
    f32 = jnp.float32
    q = jax.nn.silu((xn @ w_q).astype(f32))
    forget = lb + (1.0 - lb) * jax.nn.sigmoid((xn @ w_f).astype(f32))
    log_f = jnp.log(forget)
    k = 1.0 - forget
    v = (xn @ w_i).astype(f32)

    def chunks(t, d):
        return t.reshape(bsz, nc, HGRN_CHUNK, HGRN_HEADS, d).transpose(1, 0, 3, 2, 4)

    causal = jnp.tril(jnp.ones((HGRN_CHUNK, HGRN_CHUNK), dtype=bool))

    def step(state, inp):
        qc, kc, vc, gc = inp
        b = jnp.cumsum(gc, axis=2)
        o_inter = jnp.einsum('bhtd,bhdv->bhtv', qc * jnp.exp(b), state)
        diff = b[:, :, :, None, :] - b[:, :, None, :, :]
        decay = jnp.exp(jnp.where(causal[:, :, None], diff, -jnp.inf))
        scores = jnp.einsum('bhtd,bhsd,bhtsd->bhts', qc, kc, decay)
        o_intra = jnp.einsum('bhts,bhsv->bhtv', scores, vc)
        b_last = b[:, :, -1:, :]
        new_state = jnp.exp(b_last[:, :, 0, :])[..., None] * state + jnp.einsum(
            'bhsd,bhsv->bhdv', kc * jnp.exp(b_last - b), vc)
        return new_state, o_inter + o_intra

    state0 = jnp.zeros((bsz, HGRN_HEADS, HGRN_DK, HGRN_DV), f32)
    _, o = lax.scan(step, state0, (chunks(q, HGRN_DK), chunks(k, HGRN_DK),
                                   chunks(v, HGRN_DV), chunks(log_f, HGRN_DK)))
    o = o.transpose(1, 0, 3, 2, 4).reshape(bsz, seq, HGRN_HEADS, HGRN_DV)
    o = rmsnorm(o, g_norm)
    gate = jax.nn.silu((xn @ w_g).astype(f32)).reshape(bsz, seq, HGRN_HEADS, HGRN_DV)
    o = (o * gate).reshape(bsz, seq, D_MODEL).astype(xn.dtype)
    return o @ w_o

def shared_mla_kv(h, in_norm, w_dkv, kv_norm, w_uk, w_uv, cos, sin):
    bsz, seq, _ = h.shape
    hn = rmsnorm(h, in_norm)
    ckr = hn @ w_dkv
    c_kv = rmsnorm(ckr[..., :MLA_KV_LORA], kv_norm)
    k_rope = apply_rope(ckr[..., MLA_KV_LORA:], cos, sin)
    k_nope = (c_kv @ w_uk).reshape(bsz, seq, MLA_HEADS, MLA_NOPE)
    v = (c_kv @ w_uv).reshape(bsz, seq, MLA_HEADS, MLA_V)
    return k_nope, k_rope, v

def mla_mixer(xn, w_dq, q_norm, w_uq, w_o, k_nope, k_rope, v, cos, sin):
    bsz, seq, _ = xn.shape
    nb = seq // QBLOCK
    c_q = rmsnorm(xn @ w_dq, q_norm)
    q = (c_q @ w_uq).reshape(bsz, seq, MLA_HEADS, MLA_NOPE + MLA_ROPE)
    q_nope = q[..., :MLA_NOPE]
    q_rope = apply_rope(q[..., MLA_NOPE:], cos[:, None, :], sin[:, None, :])
    qn_b = q_nope.reshape(bsz, nb, QBLOCK, MLA_HEADS, MLA_NOPE).transpose(1, 0, 2, 3, 4)
    qr_b = q_rope.reshape(bsz, nb, QBLOCK, MLA_HEADS, MLA_ROPE).transpose(1, 0, 2, 3, 4)
    starts = jnp.arange(nb, dtype=jnp.int32) * QBLOCK
    key_pos = jnp.arange(seq, dtype=jnp.int32)
    scale = (MLA_NOPE + MLA_ROPE) ** -0.5

    def block(args):
        qn, qr, start = args
        s = jnp.einsum('bqhd,bkhd->bhqk', qn, k_nope) + jnp.einsum('bqhr,bkr->bhqk', qr, k_rope)
        s = s.astype(jnp.float32) * scale
        q_pos = start + jnp.arange(QBLOCK, dtype=jnp.int32)
        s = jnp.where(key_pos[None, :] <= q_pos[:, None], s, -jnp.inf)
        p = jax.nn.softmax(s, axis=-1).astype(v.dtype)
        return jnp.einsum('bhqk,bkhv->bqhv', p, v)

    o = lax.map(block, (qn_b, qr_b, starts))
    o = o.transpose(1, 0, 2, 3, 4).reshape(bsz, seq, MLA_HEADS * MLA_V)
    return o @ w_o

def sq_relu_mlp(xn, w_up, w_down):
    return jnp.square(jax.nn.relu(xn @ w_up)) @ w_down

def first_inputs(seed: int = 0) -> dict:
    key = jax.random.key(seed)
    ks = jax.random.split(key, 24)
    f32 = jnp.float32

    def w(k, shape, fan_in):
        return jax.random.normal(k, shape, f32) * (fan_in ** -0.5)

    def gain(k, shape):
        return 1.0 + 0.02 * jax.random.normal(k, shape, f32)

    D = D_MODEL
    return {
        'x': jax.random.normal(ks[0], (BATCH, SEQ, D), f32),
        'hgrn_norm': gain(ks[1], (N_A_LAYERS, D)),
        'hgrn_w_q': w(ks[2], (N_A_LAYERS, D, D), D),
        'hgrn_w_f': w(ks[3], (N_A_LAYERS, D, D), D),
        'hgrn_w_i': w(ks[4], (N_A_LAYERS, D, D), D),
        'hgrn_w_g': w(ks[5], (N_A_LAYERS, D, D), D),
        'hgrn_g_norm': gain(ks[6], (N_A_LAYERS, HGRN_DV)),
        'hgrn_w_o': w(ks[7], (N_A_LAYERS, D, D), D),
        'hgrn_lb_logits': 0.5 * jax.random.normal(ks[8], (N_A_LAYERS + 1, D), f32),
        'mla_norm': gain(ks[9], (N_B_LAYERS, D)),
        'mla_w_dq': w(ks[10], (N_B_LAYERS, D, MLA_Q_LORA), D),
        'mla_q_norm': gain(ks[11], (N_B_LAYERS, MLA_Q_LORA)),
        'mla_w_uq': w(ks[12], (N_B_LAYERS, MLA_Q_LORA, MLA_HEADS * (MLA_NOPE + MLA_ROPE)), MLA_Q_LORA),
        'mla_w_o': w(ks[13], (N_B_LAYERS, MLA_HEADS * MLA_V, D), MLA_HEADS * MLA_V),
        'kv_in_norm': gain(ks[14], (D,)),
        'kv_w_dkv': w(ks[15], (D, MLA_KV_LORA + MLA_ROPE), D),
        'kv_norm': gain(ks[16], (MLA_KV_LORA,)),
        'kv_w_uk': w(ks[17], (MLA_KV_LORA, MLA_HEADS * MLA_NOPE), MLA_KV_LORA),
        'kv_w_uv': w(ks[18], (MLA_KV_LORA, MLA_HEADS * MLA_V), MLA_KV_LORA),
        'mlp_norm': gain(ks[19], (DEPTH, D)),
        'mlp_w_up': w(ks[20], (DEPTH, D, D_FF), D),
        'mlp_w_down': w(ks[21], (DEPTH, D_FF, D), D_FF),
        'final_norm': gain(ks[22], (D,)),
    }

def first_block(x, hgrn_norm, hgrn_w_q, hgrn_w_f, hgrn_w_i, hgrn_w_g, hgrn_g_norm, hgrn_w_o,
              hgrn_lb_logits, mla_norm, mla_w_dq, mla_q_norm, mla_w_uq, mla_w_o,
              kv_in_norm, kv_w_dkv, kv_norm, kv_w_uk, kv_w_uv,
              mlp_norm, mlp_w_up, mlp_w_down, final_norm):
    seq = x.shape[1]
    cos, sin = rope_tables(seq)
    lower_bounds = hgrn_lower_bounds(hgrn_lb_logits)
    h = x
    k_nope = k_rope = v = None
    for l in range(DEPTH):
        if l < N_A_LAYERS:
            h = h + hgrn2_mixer(rmsnorm(h, hgrn_norm[l]), hgrn_w_q[l], hgrn_w_f[l], hgrn_w_i[l],
                                hgrn_w_g[l], hgrn_g_norm[l], hgrn_w_o[l], lower_bounds[l])
        else:
            j = l - N_A_LAYERS
            h = h + mla_mixer(rmsnorm(h, mla_norm[j]), mla_w_dq[j], mla_q_norm[j], mla_w_uq[j],
                              mla_w_o[j], k_nope, k_rope, v, cos, sin)
        h = h + sq_relu_mlp(rmsnorm(h, mlp_norm[l]), mlp_w_up[l], mlp_w_down[l])
        if l == N_A_LAYERS - 1:
            k_nope, k_rope, v = shared_mla_kv(h, kv_in_norm, kv_w_dkv, kv_norm, kv_w_uk, kv_w_uv, cos, sin)
    return rmsnorm(h, final_norm)


DEPTH_2 = 1

ATT_HEADS = 16
ATT_HEAD_DIM = 64
KV_LATENT = 128
IDX_HEADS = 8
IDX_DIM = 64
TOPK_MAX = 256
Q_BLOCK = 128
REL_BUCKETS = 32
REL_MAX_DIST = 128
SSM_INNER = 2 * D_MODEL
SSM_HEAD_DIM = 64
SSM_HEADS = SSM_INNER // SSM_HEAD_DIM
SSM_GROUPS = 4
SSM_HEADS_PER_GROUP = SSM_HEADS // SSM_GROUPS
SSM_STATE = 128
SSM_CONV = 4
SSM_CHUNK = 128
SSM_XBC = SSM_INNER + 2 * SSM_GROUPS * SSM_STATE
FFN_DIM = 2816
FFN_CONV = 3

IN_SPLITS = (
    ATT_HEADS * ATT_HEAD_DIM,
    KV_LATENT,
    IDX_HEADS * IDX_DIM,
    IDX_DIM,
    IDX_HEADS,
    SSM_INNER,
    SSM_XBC,
    SSM_HEADS,
    D_MODEL,
    D_MODEL,
)
IN_COLS = sum(IN_SPLITS)


def split_cols(a, sizes):
    idx, acc = [], 0
    for sz in sizes[:-1]:
        acc += sz
        idx.append(acc)
    return jnp.split(a, idx, axis=-1)

def rmsnorm_2(x, g):
    x32 = x.astype(jnp.float32)
    y = x32 * lax.rsqrt(jnp.mean(x32 * x32, axis=-1, keepdims=True) + EPS)
    return (y * g.astype(jnp.float32)).astype(x.dtype)

def causal_depthwise_conv(u, w, bias):
    k, ch = w.shape
    out = lax.conv_general_dilated(
        u, w[:, None, :].astype(u.dtype), window_strides=(1,), padding=[(k - 1, 0)],
        dimension_numbers=("NWC", "WIO", "NWC"), feature_group_count=ch)
    return out + bias.astype(u.dtype)

def t5_bucket(dist):
    n = jnp.maximum(dist, 0)
    max_exact = REL_BUCKETS // 2
    large = max_exact + (jnp.log(jnp.maximum(n, 1).astype(jnp.float32) / max_exact)
                         / math.log(REL_MAX_DIST / max_exact)
                         * (REL_BUCKETS - max_exact)).astype(jnp.int32)
    large = jnp.minimum(large, REL_BUCKETS - 1)
    return jnp.where(n < max_exact, n, large)

def dsa_attention(q_lat, c_kv, q_idx, k_idx, w_idx, rel_bias):
    b, s, h, c = q_lat.shape
    n_sel = min(TOPK_MAX, s // 4)
    nblk = s // Q_BLOCK
    scale = ATT_HEAD_DIM ** -0.5
    key_pos = jnp.arange(s)
    gather = jax.vmap(lambda table, idx: table[idx])

    def to_blocks(a):
        return a.reshape(b, nblk, Q_BLOCK, *a.shape[2:]).swapaxes(0, 1)

    def block(args):
        qb, qib, wib, blk = args
        q_pos = blk * Q_BLOCK + jnp.arange(Q_BLOCK)
        causal = key_pos[None, :] <= q_pos[:, None]
        idx_logits = jnp.einsum("bqhd,bsd->bqhs", qib, k_idx,
                                preferred_element_type=jnp.float32)
        score = jnp.einsum("bqhs,bqh->bqs", jax.nn.relu(idx_logits),
                           wib.astype(jnp.float32))
        score = jnp.where(causal[None], score, -jnp.inf)
        _, sel = lax.top_k(score, n_sel)
        c_sel = gather(c_kv, sel)
        logits = jnp.einsum("bqhc,bqkc->bhqk", qb, c_sel,
                            preferred_element_type=jnp.float32) * scale
        dist = q_pos[None, :, None] - sel
        bias = rel_bias[t5_bucket(dist)]
        logits = logits + jnp.moveaxis(bias, -1, 1).astype(jnp.float32)
        logits = jnp.where((dist >= 0)[:, None], logits, -jnp.inf)
        p = jax.nn.softmax(logits, axis=-1).astype(c_sel.dtype)
        return jnp.einsum("bhqk,bqkc->bqhc", p, c_sel)

    out = lax.map(block, (to_blocks(q_lat), to_blocks(q_idx), to_blocks(w_idx),
                          jnp.arange(nblk)))
    return out.swapaxes(0, 1).reshape(b, s, h, c)

def ssd_scan(xh, dt, a, bmat, cmat):
    b, l, g, r, p = xh.shape
    n = bmat.shape[-1]
    q = SSM_CHUNK
    nc = l // q
    f32 = jnp.float32
    x = (xh.astype(f32) * dt[..., None]).reshape(b, nc, q, g, r, p)
    adt = (dt * a).reshape(b, nc, q, g, r)
    bm = bmat.astype(f32).reshape(b, nc, q, g, n)
    cm = cmat.astype(f32).reshape(b, nc, q, g, n)
    a_cum = jnp.cumsum(adt, axis=2)
    tri = jnp.tril(jnp.ones((q, q), dtype=bool))
    seg = a_cum[:, :, :, None] - a_cum[:, :, None, :]
    decay = jnp.exp(jnp.where(tri[None, None, :, :, None, None], seg, -jnp.inf))
    cb = jnp.einsum("bclgn,bcsgn->bclsg", cm, bm)
    y_diag = jnp.einsum("bclsgr,bcsgrp->bclgrp", cb[..., None] * decay, x)
    decay_states = jnp.exp(a_cum[:, :, -1:] - a_cum)
    states = jnp.einsum("bclgn,bclgrp->bcgrpn", bm, x * decay_states[..., None])
    chunk_decay = jnp.exp(a_cum[:, :, -1])

    def step(hstate, inp):
        st, dec = inp
        return hstate * dec[..., None, None] + st, hstate

    h0 = jnp.zeros((b, g, r, p, n), f32)
    _, prev = lax.scan(step, h0, (states.swapaxes(0, 1), chunk_decay.swapaxes(0, 1)))
    prev = prev.swapaxes(0, 1)
    y_off = jnp.einsum("bclgn,bcgrpn->bclgrp", cm, prev) * jnp.exp(a_cum)[..., None]
    return (y_diag + y_off).reshape(b, l, g, r, p)

def gated_group_rmsnorm(y, z, g):
    u = y.astype(jnp.float32) * jax.nn.silu(z.astype(jnp.float32))
    b, l, c = u.shape
    u = u.reshape(b, l, SSM_GROUPS, c // SSM_GROUPS)
    u = u * lax.rsqrt(jnp.mean(u * u, axis=-1, keepdims=True) + EPS)
    return (u.reshape(b, l, c) * g.astype(jnp.float32)).astype(z.dtype)

def second_inputs(seed: int = 0) -> dict:
    key = jax.random.key(seed)
    ks = jax.random.split(key, 24)
    f32 = jnp.float32

    def nrm(k, shape, scale):
        return jax.random.normal(k, shape, f32) * scale

    def gain(k, shape):
        return 1.0 + 0.05 * jax.random.normal(k, shape, f32)

    dt0 = jnp.exp(jax.random.uniform(ks[8], (DEPTH_2, SSM_HEADS), f32,
                                     math.log(1e-3), math.log(1e-1)))
    dt_bias = dt0 + jnp.log(-jnp.expm1(-dt0))
    return {
        "x": nrm(ks[0], (BATCH, SEQ, D_MODEL), 1.0),
        "rel_bias": nrm(ks[1], (REL_BUCKETS, ATT_HEADS), 0.5),
        "norm_mix": gain(ks[2], (DEPTH_2, D_MODEL)),
        "w_in": nrm(ks[3], (DEPTH_2, D_MODEL, IN_COLS), D_MODEL ** -0.5),
        "kv_norm": gain(ks[4], (DEPTH_2, KV_LATENT)),
        "w_uk": nrm(ks[5], (DEPTH_2, ATT_HEADS, ATT_HEAD_DIM, KV_LATENT), ATT_HEAD_DIM ** -0.5),
        "w_uv": nrm(ks[6], (DEPTH_2, ATT_HEADS, ATT_HEAD_DIM, KV_LATENT), KV_LATENT ** -0.5),
        "conv_ssm_w": nrm(ks[7], (DEPTH_2, SSM_CONV, SSM_XBC), SSM_CONV ** -0.5),
        "conv_ssm_b": nrm(ks[9], (DEPTH_2, SSM_XBC), 0.01),
        "dt_bias": dt_bias,
        "a_log": jnp.log(jax.random.uniform(ks[10], (DEPTH_2, SSM_HEADS), f32, 1.0, 16.0)),
        "d_skip": 1.0 + 0.1 * jax.random.normal(ks[11], (DEPTH_2, SSM_HEADS), f32),
        "ssm_norm": gain(ks[12], (DEPTH_2, SSM_INNER)),
        "w_att_out": nrm(ks[13], (DEPTH_2, ATT_HEADS * ATT_HEAD_DIM, D_MODEL),
                         (ATT_HEADS * ATT_HEAD_DIM) ** -0.5),
        "w_ssm_out": nrm(ks[14], (DEPTH_2, SSM_INNER, D_MODEL), SSM_INNER ** -0.5),
        "w_out": nrm(ks[15], (DEPTH_2, D_MODEL, D_MODEL), D_MODEL ** -0.5),
        "norm_ffn": gain(ks[16], (DEPTH_2, D_MODEL)),
        "w_ffn_up": nrm(ks[17], (DEPTH_2, D_MODEL, 2 * FFN_DIM), D_MODEL ** -0.5),
        "conv_ffn_w": nrm(ks[18], (DEPTH_2, FFN_CONV, 2 * FFN_DIM), FFN_CONV ** -0.5),
        "conv_ffn_b": nrm(ks[19], (DEPTH_2, 2 * FFN_DIM), 0.01),
        "w_ffn_down": nrm(ks[20], (DEPTH_2, FFN_DIM, D_MODEL), FFN_DIM ** -0.5),
        "norm_final": gain(ks[21], (D_MODEL,)),
    }

def second_block(x, rel_bias, norm_mix, w_in, kv_norm, w_uk, w_uv, conv_ssm_w, conv_ssm_b,
              dt_bias, a_log, d_skip, ssm_norm, w_att_out, w_ssm_out, w_out, norm_ffn,
              w_ffn_up, conv_ffn_w, conv_ffn_b, w_ffn_down, norm_final):
    b, s, _ = x.shape
    for layer in range(DEPTH_2):
        h = rmsnorm_2(x, norm_mix[layer])
        proj = h @ w_in[layer]
        (q, c_raw, q_idx, k_idx, w_idx, z, xbc, dt_raw, g_att, g_ssm) = split_cols(proj, IN_SPLITS)

        q = q.reshape(b, s, ATT_HEADS, ATT_HEAD_DIM)
        q_lat = jnp.einsum("bshd,hdc->bshc", q, w_uk[layer])
        c_kv = rmsnorm_2(c_raw, kv_norm[layer])
        att_lat = dsa_attention(q_lat, c_kv,
                                q_idx.reshape(b, s, IDX_HEADS, IDX_DIM), k_idx, w_idx,
                                rel_bias)
        att = jnp.einsum("bshc,hdc->bshd", att_lat, w_uv[layer])
        y_att = att.reshape(b, s, ATT_HEADS * ATT_HEAD_DIM) @ w_att_out[layer]

        xbc = jax.nn.silu(causal_depthwise_conv(xbc, conv_ssm_w[layer], conv_ssm_b[layer]))
        xs, bm, cm = split_cols(xbc, (SSM_INNER, SSM_GROUPS * SSM_STATE, SSM_GROUPS * SSM_STATE))
        dt = jax.nn.softplus(dt_raw.astype(jnp.float32) + dt_bias[layer].astype(jnp.float32))
        a = -jnp.exp(a_log[layer].astype(jnp.float32))
        xh = xs.reshape(b, s, SSM_GROUPS, SSM_HEADS_PER_GROUP, SSM_HEAD_DIM)
        y = ssd_scan(xh,
                     dt.reshape(b, s, SSM_GROUPS, SSM_HEADS_PER_GROUP),
                     a.reshape(SSM_GROUPS, SSM_HEADS_PER_GROUP),
                     bm.reshape(b, s, SSM_GROUPS, SSM_STATE),
                     cm.reshape(b, s, SSM_GROUPS, SSM_STATE))
        y = y + d_skip[layer].astype(jnp.float32).reshape(
            SSM_GROUPS, SSM_HEADS_PER_GROUP)[..., None] * xh.astype(jnp.float32)
        y = gated_group_rmsnorm(y.reshape(b, s, SSM_INNER), z, ssm_norm[layer])
        y_ssm = y @ w_ssm_out[layer]

        merged = jax.nn.sigmoid(g_att) * y_att + jax.nn.sigmoid(g_ssm) * y_ssm
        x = x + merged @ w_out[layer]

        h = rmsnorm_2(x, norm_ffn[layer])
        u = causal_depthwise_conv(h @ w_ffn_up[layer], conv_ffn_w[layer], conv_ffn_b[layer])
        gate, val = jnp.split(u, 2, axis=-1)
        x = x + (jax.nn.silu(gate) * val) @ w_ffn_down[layer]
    return rmsnorm_2(x, norm_final)


def setup_inputs(seed=0):
    out = dict(first_inputs(seed))
    for name, value in second_inputs(seed + 1).items():
        if name != "x":
            out[name + "_2"] = value
    return out


def reference(
    x, hgrn_norm, hgrn_w_q, hgrn_w_f, hgrn_w_i, hgrn_w_g, hgrn_g_norm, hgrn_w_o, hgrn_lb_logits,
    mla_norm, mla_w_dq, mla_q_norm, mla_w_uq, mla_w_o, kv_in_norm, kv_w_dkv, kv_norm, kv_w_uk,
    kv_w_uv, mlp_norm, mlp_w_up, mlp_w_down, final_norm, rel_bias_2, norm_mix_2, w_in_2,
    kv_norm_2, w_uk_2, w_uv_2, conv_ssm_w_2, conv_ssm_b_2, dt_bias_2, a_log_2, d_skip_2,
    ssm_norm_2, w_att_out_2, w_ssm_out_2, w_out_2, norm_ffn_2, w_ffn_up_2, conv_ffn_w_2,
    conv_ffn_b_2, w_ffn_down_2, norm_final_2,
):
    x = first_block(
        x, hgrn_norm, hgrn_w_q, hgrn_w_f, hgrn_w_i, hgrn_w_g, hgrn_g_norm, hgrn_w_o,
        hgrn_lb_logits, mla_norm, mla_w_dq, mla_q_norm, mla_w_uq, mla_w_o, kv_in_norm, kv_w_dkv,
        kv_norm, kv_w_uk, kv_w_uv, mlp_norm, mlp_w_up, mlp_w_down, final_norm,
    )
    return second_block(
        x, rel_bias_2, norm_mix_2, w_in_2, kv_norm_2, w_uk_2, w_uv_2, conv_ssm_w_2,
        conv_ssm_b_2, dt_bias_2, a_log_2, d_skip_2, ssm_norm_2, w_att_out_2, w_ssm_out_2,
        w_out_2, norm_ffn_2, w_ffn_up_2, conv_ffn_w_2, conv_ffn_b_2, w_ffn_down_2, norm_final_2,
    )


_drawn_inputs = setup_inputs


def setup_inputs(seed=0):
    import zlib

    import numpy as np

    out = dict(_drawn_inputs(seed))
    spreads = {}
    factors = {'hgrn_g_norm': 3.061,
     'mla_norm': 8.0,
     'mla_q_norm': 8.0,
     'kv_in_norm': 6.525,
     'kv_norm': 6.883,
     'kv_norm_2': 4.536,
     'conv_ssm_b_2': 7.754,
     'conv_ffn_b_2': 8.0,
     'd_skip_2': 3.829,
     'ssm_norm_2': 4.352,
     'norm_ffn_2': 2.923}
    for name, (base, spread) in spreads.items():
        noise = np.random.default_rng([zlib.crc32(name.encode()), seed]).standard_normal(out[name].shape)
        drawn = base * np.exp(spread * noise) if base else spread * noise
        out[name] = __import__('jax').numpy.asarray(drawn.astype(out[name].dtype))
    for name, factor in factors.items():
        out[name] = (out[name] * factor).astype(out[name].dtype)
    return out
```

```python
from contextlib import ExitStack

import numpy as np
import concourse.bass as bass
from concourse import mybir
from concourse.alu_op_type import AluOpType as ALU

ACT = mybir.ActivationFunctionType
AX = mybir.AxisListType
F32 = mybir.dt.float32
F32R = mybir.dt.float32r
I32 = mybir.dt.int32

P = 128
D = 1024
S = 512
KT = D // P
ST = S // P
EPS = 1e-6
NEG = -1e30
TAKEN = -3e38
HEADS = 8
LEVELS = [64, 32, 16, 8, 4, 2, 1]
AHEADS = 16
MLA_SCALE = float(192) ** -0.5
D_FF = 4096
FFN = 2816
FT = FFN // P
TOPK = 128
SLOTS = 4
LOOK = SLOTS - 1
BLK = 8

STREAM = [
    ("hgrn_q", 64), ("hgrn_f", 64), ("hgrn_g", 64), ("hgrn_i", 64), ("hgrn_o", 64),
    ("mlp0_up0", 128), ("mlp0_down0", 128), ("mlp0_up1", 128), ("mlp0_down1", 128),
    ("kv", 32), ("dq", 16), ("mla", 4 * 32), ("mla_o", 128),
    ("mlp1_up0", 128), ("mlp1_down0", 128), ("mlp1_up1", 128), ("mlp1_down1", 128),
    ("dsa_in", 6 * 8), ("dsa_q", 64), ("att_out", 64), ("g_att", 64), ("xbc", 24 * 8), ("z", 128),
    ("g_ssm", 64), ("ssm_out", 128), ("w_out", 64), ("ffn_up", 2 * FT * 8), ("ffn_down", FT * 8),
]
TILES = -(-sum(n for _, n in STREAM) // (BLK * SLOTS)) * SLOTS

COLS = [
    ("ident", P), ("ones", P), ("neg", P), ("tri", P), ("flip", P), ("restart", S), ("levels", len(LEVELS) * P),
    ("hgrn_norm", 8), ("mla_norm", 8), ("kv_in_norm", 8), ("mlp_norm0", 8), ("mlp_norm1", 8),
    ("final_norm", 8), ("norm_mix", 8), ("norm_ffn", 8), ("norm_final", 8), ("g_norm", 1),
    ("lb0", 8), ("lb1", 8), ("q_norm", 2), ("kv_norm", 2), ("kv_norm2", 1), ("dt_bias", 32),
    ("a_log", 32), ("d_skip", 16), ("ssm_norm", 16), ("conv_ssm", 4 * 24), ("conv_ssm_b", 24),
    ("conv_ffn", 3 * 44), ("conv_ffn_b", 44), ("eps", 1),
]
COL = {}
NCOLS = 0
for _n, _w in COLS:
    COL[_n] = NCOLS
    NCOLS += _w
BUCKETS = 32
DISTS = 3 * P


def build(nc, stream, cols, rope, bucket, w_uk2, w_uv2, x_in, rel_bias, toep_dram, out):
    ctx = ExitStack()
    with ctx:
        BASE = 17408

        def at(name, kb, shape, dt=F32):
            return nc.alloc_sbuf_tensor_at(name, shape, dt, offset=BASE + int(kb * 1024))

        def sem(name):
            return ctx.enter_context(nc.semaphore(name))

        bank = [ctx.enter_context(nc.psum_tensor(f"bank{i}", [P, 512], F32)) for i in range(8)]

        C = at("consts", 0, [P, NCOLS])
        raw = at("w_raw", 12, [P, SLOTS, BLK * P])
        whi = at("w_hi", 28, [P, SLOTS, BLK * P], F32R)
        wlo = at("w_lo", 44, [P, SLOTS, BLK * P], F32R)
        h = at("residual", 60, [P, KT, S])
        xh = at("x_hi", 76, [P, KT, S], F32R)
        xl = at("x_lo", 92, [P, KT, S], F32R)
        sq = at("squares", 108, [P, KT, S])
        rstd = at("rstd", 124, [P, S])
        nt = at("normed", 126, [P, 4, S])

        def col(name, j=0, n=1):
            return C[:, COL[name] + j:COL[name] + j + n]

        ident, ones = col("ident", 0, P), col("ones", 0, P)

        raw_loaded = [sem(f"raw_loaded{s}") for s in range(SLOTS)]
        hi_ready = [sem(f"hi_ready{s}") for s in range(SLOTS)]
        lo_ready = sem("lo_ready")
        slots_free = sem("slots_free")
        pe_step, act_step, dve_step = sem("pe_step"), sem("act_step"), sem("dve_step")
        consts_loaded, extra_loaded, stored = sem("consts_loaded"), sem("extra_loaded"), sem("stored")
        toep_stored, toep_loaded = sem("toep_stored"), sem("toep_loaded")

        def joiner(e, mine, others):
            steps = [0]

            def join():
                steps[0] += 1
                e.drain().then_inc(mine, 1)
                for o in others:
                    e.wait_ge(o, steps[0])
            return join

        block = ctx.enter_context(nc.Block())

        class Flow:

            def __init__(self, name, more=""):
                self.full = sem(name + "_full")
                self.free = sem(name + "_free")
                self.a = sem(name + "_act") if "a" in more else None
                self.b = sem(name + "_dve") if "b" in more else None
                self.c = sem(name + "_gated") if "c" in more else None

        class Norm:

            def __init__(self, src, gain, oh=None, ol=None, o32=None, sq=sq, rstd=rstd):
                self.sqb, self.rs = sq, rstd
                self.src, self.gain, self.oh, self.ol, self.o32 = src, gain, oh, ol, o32
                self.tiles0, self.split0, self.norm0 = norm_counts
                norm_counts[0] += len(src)
                norm_counts[1] += len(src) if oh else 0
                norm_counts[2] += 1

        norm_counts = [0, 0, 0]
        norm_sq, norm_sum, norm_rstd = sem("norm_squares"), sem("norm_sum"), sem("norm_rstd")
        norm_tile, norm_hi = sem("norm_tile"), sem("norm_hi")

        def tiles(t, n, first=0):
            return [t[:, first + j, :] for j in range(n)]

        def gains(name, n):
            return [col(name, j) for j in range(n)]

        def norm_pe(e, n, b=0):
            k = len(n.src)
            for j in range(k):
                e.wait_ge(norm_sq, n.tiles0 + j + 1)
                mm = e.matmul(bank[b][:, :], ones, n.sqb[:, j, :], start=j == 0, stop=j == k - 1)
            mm.then_inc(norm_sum, 1)

        def norm_act(e, n, b=0):
            k = len(n.src)
            for j in range(k):
                e.activation(n.sqb[:, j, :], n.src[j], ACT.Square).then_inc(norm_sq, 1)
            e.wait_ge(norm_sum, n.norm0 + 1)
            e.activation(n.rs[:, :], bank[b][:, :], ACT.Ln, scale=1.0 / (k * P), bias=col("eps"))
            e.drain()
            e.activation(n.rs[:, :], n.rs[:, :], ACT.Exp, scale=-0.5).then_inc(norm_rstd, 1)
            if n.oh is not None:
                for j in range(k):
                    e.wait_ge(norm_tile, n.split0 + j + 1)
                    e.activation(n.oh[j], nt[:, j % 4, :], ACT.Copy).then_inc(norm_hi, 1)

        def norm_dve(e, n):
            k = len(n.src)
            e.wait_ge(norm_rstd, n.norm0 + 1)
            if n.oh is None:
                for j in range(k):
                    e.scalar_tensor_tensor(n.o32[j], n.src[j], n.gain[j], n.rs[:, :], ALU.mult, ALU.mult)
                return

            def low(j):
                e.wait_ge(norm_hi, n.split0 + j + 1)
                e.tensor_tensor(n.ol[j], nt[:, j % 4, :], n.oh[j].bitcast(F32), ALU.subtract)

            for j in range(k):
                e.scalar_tensor_tensor(nt[:, j % 4, :], n.src[j], n.gain[j], n.rs[:, :],
                                       ALU.mult, ALU.mult).then_inc(norm_tile, 1)
                if j >= 1:
                    low(j - 1)
            e.drain()
            low(k - 1)

        class Split:

            def __init__(self, name, src, oh, ol):
                self.src, self.oh, self.ol, self.hi = src, oh, ol, sem(name + "_hi")

        def split_act(e, s):
            for src, oh in zip(s.src, s.oh):
                e.activation(oh, src, ACT.Copy).then_inc(s.hi, 1)

        def split_dve(e, s):
            for j, (src, oh, ol) in enumerate(zip(s.src, s.oh, s.ol)):
                e.wait_ge(s.hi, j + 1)
                e.tensor_tensor(ol, src, oh.bitcast(F32), ALU.subtract)

        hq, hk = at("hgrn_q", 108, [P, HEADS, S]), at("hgrn_k", 124, [P, HEADS, S])
        hb, hv = at("hgrn_logf", 140, [P, HEADS, S]), at("hgrn_v", 156, [P, ST, D])
        hg, ht = at("hgrn_gate", 172, [P, HEADS, S]), at("hgrn_t", 188, [P, HEADS, S])
        hx, hs = at("hgrn_x", 76, [P, HEADS, S]), at("hgrn_scores", 92, [P, HEADS, S])
        htmp = at("hgrn_tmp", 188, [P, 4, S])
        lb, oml = at("hgrn_lb", 204, [P, 8]), at("hgrn_oml", 204.25, [P, 8])
        lbt = at("hgrn_lbt", 204.5, [P, 3, 8])
        ebl = at("hgrn_ebl", 205, [P, HEADS * ST])

        HH = D_FF // P // 2
        uh, ul = at("hidden_hi", 108, [P, HH, S], F32R), at("hidden_lo", 140, [P, HH, S], F32R)
        ur, ut = at("relu", 172, [P, 4, S]), at("relu_sq", 180, [P, 4, S])

        ckv, cq = at("mla_ckv", 134, [P, 2, S]), at("mla_cq", 138, [P, 2, S])
        ckh, ckl = at("mla_ckv_hi", 142, [P, 2, S], F32R), at("mla_ckv_lo", 146, [P, 2, S], F32R)
        cqh, cql = at("mla_cq_hi", 150, [P, 2, S], F32R), at("mla_cq_lo", 154, [P, 2, S], F32R)
        kr, rp = at("mla_k_rope", 158, [P, 2, S]), at("rope_table", 162, [P, 2, S])
        rt = at("rope_tmp", 166, [P, 4, S])
        mo = at("mla_o", 174, [P, AHEADS, S])
        gk, gq = at("mla_gk", 76, [P, 4, S]), at("mla_gq", 84, [P, 4, S])
        gr, gv = at("mla_gq_rope", 92, [P, 2, S]), at("mla_gv", 96, [P, ST, 4 * P])
        moh, mol = at("mla_o_hi", 76, [P, AHEADS, S], F32R), at("mla_o_lo", 108, [P, AHEADS, S], F32R)
        pr, pt = at("probs", 104, [P, 3, S]), at("probs_t", 110, [P, ST, S])
        lg = at("logits", 118, [P, 2, S])
        mx, nm = at("row_max", 122, [P, 64]), at("neg_max", 122.25, [P, 64])
        rs, ri = at("row_sum", 122.5, [P, 64]), at("row_inv", 122.75, [P, 64])

        AOFF = 28
        pr2, pt2 = at("probs2", 104 + AOFF, [P, 3, S]), at("probs_t2", 110 + AOFF, [P, ST, S])
        lg2 = at("logits2", 118 + AOFF, [P, 2, S])
        mx2, nm2 = at("row_max2", 122 + AOFF, [P, 64]), at("neg_max2", 122.25 + AOFF, [P, 64])
        rs2, ri2 = at("row_sum2", 122.5 + AOFF, [P, 64]), at("row_inv2", 122.75 + AOFF, [P, 64])
        dq2 = at("dsa_q", 151, [P, 8, S])
        dql, dlo = at("dsa_qlat", 167, [P, 4, S]), at("dsa_lat", 175, [P, 4, S])
        dc, dcn = at("dsa_c", 183, [P, S]), at("dsa_c_nat", 185, [P, ST, P])
        dsm = at("dsa_selected", 187, [P, ST, S])
        tp = at("toeplitz", 108, [P, AHEADS, 2 * P])
        dnat = at("small_nat", 204, [P, ST, P])
        dqi, dki = at("dsa_qidx", 132, [P, 4, S]), at("dsa_kidx", 140, [P, S])
        dsmall, dcraw = at("dsa_small", 142, [P, S]), at("dsa_craw", 144, [P, S])
        dre = at("dsa_relu", 167, [P, 4, S])
        dsc, dwk = at("dsa_score", 175, [P, 3, S]), at("dsa_work", 126, [P, 3, S])
        dm8 = at("dsa_max8", 181, [P, 3, 8])
        drow = at("dsa_bias_row", 181.25, [AHEADS, DISTS])
        wuk, wuv = at("dsa_wuk", 195, [P, 8, P]), at("dsa_wuv", 199, [P, AHEADS, 64])
        boh, rb = at("bucket_onehot", 146, [BUCKETS, DISTS]), at("rel_bias", 147.5, [BUCKETS, AHEADS])
        ath, atl = at("att_hi", 108, [P, 8, S], F32R), at("att_lo", 124, [P, 8, S], F32R)
        mg = at("merged", 188, [P, 8, S])
        gsig = at("gate_sig", 140, [P, 4, S])

        xbc = at("ssm_xbc", 108, [P, 24, S])
        xs = xbc
        cu, ca = at("conv_in", 156, [P, 2, S + 4]), at("conv_acc", 160.25, [P, 4, S])
        cs = at("conv_sig", 168.25, [P, 2, S])
        sdt, sad = at("ssm_dt", 156, [P, ST, 32]), at("ssm_adt", 156.5, [P, ST, 32])
        sac, sat = at("ssm_acum", 157, [P, ST, 32]), at("ssm_atot", 157.5, [P, ST, 32])
        sds, scd = at("ssm_decay_states", 158, [P, ST, 32]), at("ssm_chunk_decay", 158.5, [P, ST, 32])
        sam = at("ssm_a", 159, [P, 32])
        sact = at("ssm_acum_t", 159.25, [32, S])
        sxn, sbn = at("ssm_x_nat", 161.25, [P, ST, S]), at("ssm_b_nat", 169.25, [P, ST, P])
        scb, sgt = at("ssm_cb", 171.25, [P, ST, P]), at("ssm_g", 173.25, [P, 2, S])
        sst, sxd = at("ssm_state", 177.25, [P, 3, S]), at("ssm_xd", 183.25, [P, S])
        sz = at("ssm_softplus", 177.25, [P, 6, P])
        sea = at("ssm_exp_a", 185.25, [P, S])
        gss = at("gate_ssm", 140, [P, 8, S])
        zt = at("z_tmp", 156, [P, 4, S])
        gsq, grs = at("ssm_squares", 156, [P, 4, S]), at("ssm_rstd", 164, [P, S])
        yh, yl = at("y_hi", 76, [P, 16, S], F32R), at("y_lo", 156, [P, 16, S], F32R)

        fh, fl = at("ffn_hi", 108, [P, FT, S], F32R), at("ffn_lo", 152, [P, FT, S], F32R)
        fu, fa = at("ffn_in", 196, [P, S + 4]), at("ffn_gate", 198.25, [P, S])
        fv, fs = at("ffn_val", 200.25, [P, S]), at("ffn_sig", 202.25, [P, S])

        @block.sync
        def _(e):
            e.dma_start(C[:, :], cols).then_inc(consts_loaded, 16)
            e.dma_start(h[:, :, :], x_in).then_inc(consts_loaded, 16)
            for s in range(SLOTS):
                e.dma_start(raw[:, s, :], stream[s]).then_inc(raw_loaded[s], 16)
            with e.Fori(1, TILES // SLOTS) as i:
                for s in range(SLOTS):
                    e.wait_ge(lo_ready, SLOTS * i + (s + 1 - SLOTS))
                    e.dma_start(raw[:, s, :], stream[SLOTS * i + s]).then_inc(raw_loaded[s], 16)

        @block.gpsimd
        def _(e):
            def may_cast(s, turn, tile):
                e.wait_ge(raw_loaded[s], 16 * turn + 16)
                e.wait_ge(slots_free, tile + 1)

            def cast(s):
                e.dma_start(whi[:, s, :], raw[:, s, :]).then_inc(hi_ready[s], 16)

            def low(s, turn):
                e.wait_ge(hi_ready[s], 16 * turn + 16)
                e.tensor_tensor(wlo[:, s, :], raw[:, s, :], whi[:, s, :].bitcast(F32),
                                ALU.subtract).then_inc(lo_ready, 1)

            for s in range(2):
                may_cast(s, 0, s)
                cast(s)
            last = TILES // SLOTS - 1
            with e.Fori(0, last) as i:
                for s in range(SLOTS):
                    n = (s + 2) % SLOTS
                    may_cast(n, i + (s + 2) // SLOTS, SLOTS * i + (s + 2))
                    low(s, i)
                    cast(n)
            for s in range(SLOTS):
                if s < 2:
                    may_cast(s + 2, last, SLOTS * last + s + 2)
                low(s, last)
                if s < 2:
                    cast(s + 2)

        flow = {n: Flow(n, more) for n, more in (
            ("hgrn_q", "a"), ("hgrn_f", "a"), ("hgrn_g", "a"), ("hgrn_o", ""), ("mlp0_up0", "ab"),
            ("mlp0_down0", ""), ("mlp0_up1", "ab"), ("mlp0_down1", ""), ("kv", ""), ("dq", ""),
            ("mla_o", ""), ("mlp1_up0", "ab"), ("mlp1_down0", ""), ("mlp1_up1", "ab"),
            ("mlp1_down1", ""), ("dsa_in", ""), ("dsa_q", ""), ("att_out", ""), ("g_att", "a"),
            ("xbc", "ab"), ("z", "a"), ("g_ssm", ""), ("ssm_out", ""), ("w_out", ""),
            ("ffn_up", "abc"), ("ffn_down", ""))}

        def weight_reader(e):
            pos = [0]

            class Reader:
                fresh = False

                def block(self, i=None, stride=0):
                    s, b = (pos[0] // BLK) % SLOTS, pos[0] % BLK
                    if b == 0:
                        tile = pos[0] // BLK
                        e.wait_ge(lo_ready, (tile + 1) if i is None else stride * i + (tile + 1))
                        self.fresh = True
                    pos[0] += 1
                    return whi[:, s, b * P:(b + 1) * P], wlo[:, s, b * P:(b + 1) * P]

                def at_tile_start(self, mm):
                    if self.fresh:
                        mm.then_inc(slots_free, 1)
                        self.fresh = False

                def tile(self):
                    s = (pos[0] // BLK) % SLOTS
                    for _ in range(BLK):
                        self.block()
                    return s

                def skip(self, n):
                    pos[0] += n
            return Reader()

        def product(e, w, out, rh, rl, first, last, i=None, stride=0):
            wh, wl = w.block(i, stride)
            mm = e.matmul(out, wh, rh, start=first, stop=False)
            w.at_tile_start(mm)
            e.matmul(out, wh, rl, start=False, stop=False)
            return e.matmul(out, wl, rh, start=False, stop=last)

        def linear_pe(e, w, f, rh, rl, kb, mt, body, banks=4):
            iters = mt // body

            def tiles_of(i):
                for m in range(body):
                    e.wait_ge(f.free, (m + 1) if i is None else body * i + (m + 1))
                    for k in range(kb):
                        mm = product(e, w, bank[m % banks][:, :], rh[:, k, :], rl[:, k, :],
                                     k == 0, k == kb - 1, i, body * kb // BLK)
                    mm.then_inc(f.full, 1)

            if iters == 1:
                tiles_of(None)
            else:
                with e.Fori(0, iters) as i:
                    tiles_of(i)
                w.skip((iters - 1) * body * kb)

        def looped(e, mt, body, step):
            with e.Fori(0, mt // body) as i:
                for m in range(body):
                    step(body * i + m, m)

        def banks_are_free(e, f, n=4):
            e.drain().then_inc(f.free, n)

        norms = {
            "hgrn": Norm(tiles(h, 8), gains("hgrn_norm", 8), tiles(xh, 8), tiles(xl, 8)),
            "mlp0": Norm(tiles(h, 8), gains("mlp_norm0", 8), tiles(xh, 8), tiles(xl, 8)),
            "kv": Norm(tiles(h, 8), gains("kv_in_norm", 8), tiles(xh, 8), tiles(xl, 8)),
            "ckv": Norm(tiles(ckv, 2), gains("kv_norm", 2), tiles(ckh, 2), tiles(ckl, 2)),
            "mla": Norm(tiles(h, 8), gains("mla_norm", 8), tiles(xh, 8), tiles(xl, 8)),
            "cq": Norm(tiles(cq, 2), gains("q_norm", 2), tiles(cqh, 2), tiles(cql, 2)),
            "mlp1": Norm(tiles(h, 8), gains("mlp_norm1", 8), tiles(xh, 8), tiles(xl, 8)),
            "final": Norm(tiles(h, 8), gains("final_norm", 8), o32=tiles(h, 8)),
            "mix": Norm(tiles(h, 8), gains("norm_mix", 8), tiles(xh, 8), tiles(xl, 8)),
            "c2": Norm([dcraw[:, :]], gains("kv_norm2", 1), o32=[dc[:, :]]),
        }
        split_mo = Split("s_mo", tiles(mo, 16), tiles(moh, 16), tiles(mol, 16))
        split_att = Split("s_att", tiles(dq2, 8), tiles(ath, 8), tiles(atl, 8))
        split_y = Split("s_y", tiles(xs, 16), tiles(yh, 16), tiles(yl, 16))
        split_mg = Split("s_mg", tiles(mg, 8), tiles(xh, 8), tiles(xl, 8))
        norms_y = [Norm(tiles(xs, 4, 4 * g), [col("ssm_norm", 4 * g + j) for j in range(4)],
                        o32=tiles(xs, 4, 4 * g), sq=gsq, rstd=grs) for g in range(4)]
        norms["ffn"] = Norm(tiles(h, 8), gains("norm_ffn", 8), tiles(xh, 8), tiles(xl, 8))
        norms["last"] = Norm(tiles(h, 8), gains("norm_final", 8), o32=tiles(h, 8))
        split_og = Split("s_og", tiles(hk, 8), tiles(xh, 8), tiles(xl, 8))
        v_full = sem("v_full")
        lvl_diff, lvl_exp = sem("lvl_diff"), sem("lvl_exp")
        lvl_x, lvl_mm = sem("lvl_x"), sem("lvl_mm")
        st_pe, st_dve = sem("state_pe"), sem("state_dve")
        og_sq, og_sum, og_r = sem("og_sq"), sem("og_sum"), sem("og_r")
        og_t, og_hi = sem("og_t"), sem("og_hi")
        at_s, at_m, at_e = sem("scores_full"), sem("neg_max_ready"), sem("exp_done")
        at_p, at_t, at_c = sem("probs_ready"), sem("probs_t_full"), sem("probs_t_copied")
        at_o, at_oc = sem("attn_out_full"), sem("attn_out_copied")
        ix_full, ix_relu, ix_used = sem("idx_full"), sem("idx_relu"), sem("idx_used")
        flip_full = sem("flip_full")
        sg_sel, sg_sub, sg_exp = sem("ssm_rows_full"), sem("ssm_diff"), sem("ssm_exp")
        sg_g, sg_y, sg_yd = sem("ssm_g_ready"), sem("ssm_y_full"), sem("ssm_y_done")

        def chunk(c):
            return slice(c * P, (c + 1) * P)

        def four(x):
            return x.rearrange("p (c t) -> p c t", c=ST)

        def to_four(x):
            return x.unsqueeze(1).broadcast_to([P, ST, P])

        def heads_out(x, n):
            return x.unsqueeze(2).broadcast_to([P, n, 64])

        mla = dict(p=pr, pt=pt, mx=mx, nm=nm, rs=rs, ri=ri, scale=MLA_SCALE, first=0)
        dsa = dict(p=pr2, pt=pt2, mx=mx2, nm=nm2, rs=rs2, ri=ri2, scale=1.0, first=64)
        ITEMS = 16

        def attention_pe(e, a, g, scores, value):
            n0 = a["first"] + ITEMS * g
            h0 = n0 // 4

            def out_product(hh):
                e.wait_ge(at_c, n0 + 4 * hh + 4)
                if hh >= 2:
                    e.wait_ge(at_oc, h0 + hh - 1)
                for k in range(ST):
                    mm = e.matmul(bank[5 + hh % 2][:, k * P:], value(hh, k), a["pt"][:, k, k * P:],
                                  start=k == 0, stop=k == ST - 1)
                mm.then_inc(at_o, 1)

            for n in range(ITEMS + 2):
                if n < ITEMS:
                    if n >= 3:
                        e.wait_ge(at_e, n0 + n - 2)
                    scores(n // 4, n % 4, bank[n % 3]).then_inc(at_s, 1)
                m = n - 2
                if m >= 4 and m % 4 == 0:
                    out_product(m // 4 - 1)
                if m >= 0:
                    e.wait_ge(at_p, n0 + m + 1)
                    if m >= 2:
                        e.wait_ge(at_c, n0 + m - 1)
                    for k in range(m % 4 + 1):
                        mm = e.transpose(bank[3 + m % 2][:, chunk(k)], a["p"][:, m % 3, chunk(k)], ident)
                    mm.then_inc(at_t, 1)
            out_product(3)

        def attention_act(e, a, g, logits):
            n0 = a["first"] + ITEMS * g
            h0 = n0 // 4
            for n in range(ITEMS + 2):
                if n < ITEMS:
                    w = (n % 4 + 1) * P
                    q = (n0 + n) % 64
                    e.wait_ge(at_m, n0 + n + 1)
                    if n >= 3:
                        e.wait_ge(at_t, n0 + n - 2)
                    e.activation(a["p"][:, n % 3, 0:w], logits(n)[:, 0:w], ACT.Exp, scale=a["scale"],
                                 bias=a["nm"][:, q:q + 1],
                                 accum_out=a["rs"][:, q:q + 1]).then_inc(at_e, 1)
                m = n - 2
                if m >= 0:
                    i = m % 4
                    e.wait_ge(at_t, n0 + m + 1)
                    if i == 0 and m >= 4:
                        e.wait_ge(at_o, h0 + m // 4)
                    e.activation(a["pt"][:, 0:i + 1, chunk(i)],
                                 bank[3 + m % 2][:, 0:(i + 1) * P].rearrange("p (k q) -> p k q", q=P),
                                 ACT.Copy).then_inc(at_c, 1)

        def attention_dve(e, a, g, logits, out):
            n0 = a["first"] + ITEMS * g
            h0 = n0 // 4

            def copy_out(hh):
                e.wait_ge(at_o, h0 + hh + 1)
                e.tensor_copy(out(hh), bank[5 + hh % 2][:, :]).then_inc(at_oc, 1)

            for n in range(ITEMS + 1):
                if n < ITEMS:
                    w = (n % 4 + 1) * P
                    q = (n0 + n) % 64
                    e.wait_ge(at_s, n0 + n + 1)
                    src = logits(e, n)
                    e.reduce_max(a["mx"][:, q:q + 1], src[:, 0:w], axis=AX.X)
                    e.drain()
                    e.tensor_scalar(a["nm"][:, q:q + 1], a["mx"][:, q:q + 1], -a["scale"], None,
                                    ALU.mult).then_inc(at_m, 1)
                m = n - 1
                if m >= 0:
                    w = (m % 4 + 1) * P
                    q = (n0 + m) % 64
                    e.wait_ge(at_e, n0 + m + 1)
                    e.reciprocal(a["ri"][:, q:q + 1], a["rs"][:, q:q + 1])
                    e.drain()
                    e.tensor_scalar(a["p"][:, m % 3, 0:w], a["p"][:, m % 3, 0:w], a["ri"][:, q:q + 1],
                                    None, ALU.mult).then_inc(at_p, 1)
                if n >= 7 and (n - 7) % 4 == 0:
                    copy_out((n - 7) // 4)
            copy_out(3)

        def half(x, L):
            return x[:, :, :].rearrange("p h (n u l) -> p (h n) u l", u=2, l=L)

        @block.tensor
        def _(e):
            join = joiner(e, pe_step, (act_step, dve_step))
            w = weight_reader(e)
            e.drain().then_inc(slots_free, LOOK)
            e.wait_ge(consts_loaded, 32)

            def norm(name):
                norm_pe(e, norms[name])
                join()

            def lin(name, rh, rl, kb, mt, body):
                linear_pe(e, w, flow[name], rh, rl, kb, mt, body)
                join()

            join()
            join()
            norm("hgrn")
            lin("hgrn_q", xh, xl, 8, 8, 4)
            lin("hgrn_f", xh, xl, 8, 8, 4)
            lin("hgrn_g", xh, xl, 8, 8, 4)
            for k in range(8):
                s = w.tile()
                wh, wl = whi[:, s, :], wlo[:, s, :]
                for t in range(ST):
                    for n in range(2):
                        o = bank[2 * t + n][:, :]
                        mm = e.matmul(o, xh[:, k, chunk(t)], wh[:, n * 512:(n + 1) * 512], start=k == 0, stop=False)
                        w.at_tile_start(mm)
                        e.matmul(o, xl[:, k, chunk(t)], wh[:, n * 512:(n + 1) * 512], start=False, stop=False)
                        mm = e.matmul(o, xh[:, k, chunk(t)], wl[:, n * 512:(n + 1) * 512], start=False, stop=k == 7)
            mm.then_inc(v_full, 1)
            join()
            join()
            join()
            join()
            for hh in range(HEADS):
                for c in range(ST):
                    mm = e.matmul(bank[hh][:, chunk(c)], hk[:, hh, chunk(c)], hq[:, hh, chunk(c)],
                                  start=True, stop=True)
            mm.then_inc(lvl_mm, 1)
            for n in range(len(LEVELS)):
                x = (hx, ht)[n % 2]
                e.wait_ge(lvl_x, n + 1)
                for hh in range(HEADS):
                    for c in range(ST):
                        mm = e.matmul(bank[hh][:, chunk(c)], x[:, hh, chunk(c)], x[:, hh, chunk(c)],
                                      start=True, stop=True)
                mm.then_inc(lvl_mm, 1)
            join()
            join()
            join()
            join()
            for hh in range(HEADS):
                for c in range(ST):
                    mm = e.transpose(bank[hh][:, chunk(c)], ht[:, hh, chunk(c)], ident)
            join()
            join()
            for g in range(2):
                for c in range(ST):
                    for j in range(4):
                        hh = 4 * g + j
                        e.matmul(bank[j][:, chunk(c)], hv[:, c, chunk(hh)], hs[:, hh, chunk(c)],
                                 start=True, stop=c == 0)
                        state = ht[:, hh // 4, chunk(hh % 4)]
                        if c:
                            e.wait_ge(st_dve, 12 * g + 4 * (c - 1) + j + 1)
                            e.matmul(bank[j][:, chunk(c)], state, hx[:, hh, chunk(c)], start=False, stop=True)
                        if c < ST - 1:
                            e.matmul(bank[4 + j][:, chunk(c)], hb[:, hh, chunk(c)], hv[:, c, chunk(hh)],
                                     start=True, stop=True).then_inc(st_pe, 1)
                join()
                join()
            join()
            for hh in range(HEADS):
                e.matmul(bank[hh][:, :], ones, hx[:, hh, :], start=True, stop=True).then_inc(og_sum, 1)
            join()
            join()
            join()
            lin("hgrn_o", xh, xl, 8, 8, 4)

            def mlp(n):
                norm(f"mlp{n}")
                for k in range(2):
                    lin(f"mlp{n}_up{k}", xh, xl, 8, 16, 4)
                    lin(f"mlp{n}_down{k}", uh, ul, 16, 8, 4)

            mlp(0)
            norm("kv")
            lin("kv", xh, xl, 8, 4, 4)
            norm("ckv")
            norm("mla")
            lin("dq", xh, xl, 8, 2, 2)
            norm("cq")
            for g in range(4):
                for j in range(4):
                    for k in range(2):
                        product(e, w, bank[j][:, :], ckh[:, k, :], ckl[:, k, :], k == 0, k == 1)
                for j in range(4):
                    for k in range(2):
                        product(e, w, bank[4 + j][:, :], cqh[:, k, :], cql[:, k, :], k == 0, k == 1)
                join()
                join()
                for j in range(2):
                    for k in range(2):
                        product(e, w, bank[j][:, :], cqh[:, k, :], cql[:, k, :], k == 0, k == 1)
                w.skip(4)
                s = w.tile()
                for k in range(2):
                    off = 512 * k
                    for t in range(ST):
                        o = bank[2 + t][:, :]
                        mm = e.matmul(o, ckh[:, k, chunk(t)], whi[:, s, off:off + 512], start=k == 0, stop=False)
                        w.at_tile_start(mm)
                        e.matmul(o, ckl[:, k, chunk(t)], whi[:, s, off:off + 512], start=False, stop=False)
                        e.matmul(o, ckh[:, k, chunk(t)], wlo[:, s, off:off + 512], start=False, stop=k == 1)
                join()
                join()

                def scores(j, i, b):
                    n = (i + 1) * P
                    r = slice(32 * j, 32 * j + 32)
                    e.matmul(b[:, 0:n], gq[:, j, chunk(i)], gk[:, j, 0:n], start=True, stop=False)
                    e.matmul(b[:, 0:n], gr[r, 0, chunk(i)], kr[r, 0, 0:n], start=False, stop=False)
                    e.matmul(b[:, 0:n], gr[r, 1, chunk(i)], kr[r, 1, 0:n], start=False, stop=False)
                    return e.matmul(b[:, chunk(i)], ident, col("neg", 0, P), start=False, stop=True)

                attention_pe(e, mla, g, scores, lambda j, k: gv[:, k, chunk(j)])
                join()
            join()
            lin("mla_o", moh, mol, 16, 8, 4)
            mlp(1)
            norm("final")
            norm("mix")
            lin("dsa_in", xh, xl, 8, 6, 6)
            lin("dsa_q", xh, xl, 8, 8, 4)
            norm("c2")
            for c in range(ST):
                e.transpose(bank[0][:, chunk(c)], dsmall[:, chunk(c)], ident)
                e.transpose(bank[1][:, chunk(c)], dc[:, chunk(c)], ident)
            e.wait_ge(extra_loaded, 16 * 5)
            e.matmul(bank[2][0:AHEADS, 0:DISTS], rb[:, :], boh[:, :], start=True, stop=True)
            join()
            join()
            for i in range(1, ST):
                for j in range(8):
                    n = 8 * (i - 1) + j
                    r = slice(64 * (j % 2), 64 * (j % 2) + 64)
                    if n >= 4:
                        e.wait_ge(ix_relu, n - 3)
                    e.matmul(bank[n % 4][:, 0:(i + 1) * P], dqi[r, j // 2, chunk(i)], dki[r, 0:(i + 1) * P],
                             start=True, stop=True).then_inc(ix_full, 1)
            e.wait_ge(ix_relu, 24)
            e.wait_ge(toep_loaded, 16)
            for b in range(8):
                mm = e.matmul(bank[b][:, :], col("flip", 0, P),
                              tp[:, 2 * b:2 * b + 2, :].rearrange("p h j -> p (h j)"), start=True, stop=True)
            mm.then_inc(flip_full, 1)
            join()
            for g in range(4):
                for j in range(4):
                    hh = 4 * g + j
                    r = slice(64 * (hh % 2), 64 * (hh % 2) + 64)
                    e.matmul(bank[j][:, :], wuk[r, hh // 2, :], dq2[r, hh // 2, :], start=True, stop=True)
                join()
                join()
                attention_pe(e, dsa, g,
                             lambda j, i, b: e.matmul(b[:, 0:(i + 1) * P], dql[:, j, chunk(i)],
                                                      dc[:, 0:(i + 1) * P], start=True, stop=True),
                             lambda j, k: dcn[:, k, :])
                join()
                for j in range(4):
                    e.matmul(bank[j // 2][64 * (j % 2):64 * (j % 2) + 64, :], wuv[:, 4 * g + j, :],
                             dlo[:, j, :], start=True, stop=True)
                join()
                join()
            join()
            lin("att_out", ath, atl, 8, 8, 4)
            lin("g_att", xh, xl, 8, 8, 4)
            lin("xbc", xh, xl, 8, 24, 4)
            join()
            join()
            join()
            for c in range(ST):
                e.matmul(bank[0][:, c * 32:(c + 1) * 32], col("tri", 0, P), sad[:, c, :], start=True, stop=True)
                e.matmul(bank[1][:, c * 32:(c + 1) * 32], ones, sad[:, c, :], start=True, stop=True)
                e.matmul(bank[2][0:32, chunk(c)], sad[:, c, :], col("tri", 0, P), start=True, stop=True)
            join()
            join()
            join()
            for g in range(4):
                for c in range(ST):
                    for t in range(4):
                        e.transpose(bank[c][:, chunk(t)], xbc[:, 4 * g + t, chunk(c)], ident)
                    e.transpose(bank[4][:, chunk(c)], xbc[:, 16 + g, chunk(c)], ident)
                    e.matmul(bank[5][:, chunk(c)], xbc[:, 16 + g, chunk(c)], xbc[:, 20 + g, chunk(c)],
                             start=True, stop=True)
                join()
                join()
                for c in range(ST - 1):
                    e.wait_ge(st_dve, 24 + 3 * g + c + 1)
                    e.matmul(bank[c][:, :], sbn[:, c, :], sxd[:, :], start=True, stop=True).then_inc(st_pe, 1)
                join()

                def rows(p):
                    if p >= 1:
                        e.wait_ge(sg_sub, 2 * (4 * g + p))
                        e.wait_ge(sg_exp, 3 * (4 * g + p))
                    hh = 8 * g + 2 * p
                    for q in range(2):
                        e.matmul(bank[q][:, :], ident[0:32, hh + q:hh + q + 1].broadcast_to([32, P]),
                                 sact[:, :], start=True, stop=True)
                    for q in range(2):
                        mm = e.matmul(bank[2][64 * q:64 * q + 64, :],
                                      ident[0:32, hh + q:hh + q + 1].broadcast_to([32, 64]),
                                      sact[:, :], start=True, stop=True)
                    mm.then_inc(sg_sel, 1)

                rows(0)
                for p in range(4):
                    if p < 3:
                        rows(p + 1)
                    n = 4 * g + p
                    if p:
                        e.wait_ge(sg_yd, n)
                    e.wait_ge(sg_g, n + 1)
                    for q in range(2):
                        o = slice(64 * q, 64 * q + 64)
                        for c in range(ST):
                            e.matmul(bank[4][o, chunk(c)], sxn[:, c, 128 * p + 64 * q:128 * p + 64 * q + 64],
                                     sgt[:, q, chunk(c)], start=True, stop=True)
                    for c in range(1, ST):
                        mm = e.matmul(bank[5][:, chunk(c)], sst[:, c - 1, chunk(p)],
                                      xbc[:, 20 + g, chunk(c)], start=True, stop=True)
                    mm.then_inc(sg_y, 1)
                join()
            lin("z", xh, xl, 8, 16, 4)
            lin("g_ssm", xh, xl, 8, 8, 4)
            for g in range(4):
                norm_pe(e, norms_y[g])
                join()
            join()
            lin("ssm_out", yh, yl, 16, 8, 4)
            join()
            lin("w_out", xh, xl, 8, 8, 4)
            norm("ffn")
            lin("ffn_up", xh, xl, 8, 44, 4)
            lin("ffn_down", fh, fl, FT, 8, 8)
            norm("last")

        @block.scalar
        def _(e):
            join = joiner(e, act_step, (pe_step, dve_step))
            e.wait_ge(consts_loaded, 32)

            def norm(name):
                norm_act(e, norms[name])
                join()

            def gate(name, mt, dst):
                f = flow[name]

                def step(m, j):
                    e.wait_ge(f.full, m + 1)
                    e.wait_ge(f.free, m + 1)
                    e.activation(dst[:, j, :], bank[j][:, :], ACT.Sigmoid).then_inc(f.a, 1)
                looped(e, mt, 4, step)
                join()

            def copies(name, outs, scale=1.0):
                f = flow[name]
                banks_are_free(e, f)
                for m, places in enumerate(outs):
                    e.wait_ge(f.full, m + 1)
                    for k, (rows, dst) in enumerate(places):
                        mm = e.activation(dst, bank[m % 4][rows, :], ACT.Copy, scale=scale)
                    mm.then_inc(f.free, 1)
                join()

            def whole(dst):
                return [(slice(0, P), dst)]

            join()
            e.activation(lbt[:, 0:2, :], lbt[:, 0:2, :], ACT.Exp)
            join()
            norm("hgrn")
            gate("hgrn_q", 8, htmp)
            gate("hgrn_f", 8, htmp)
            gate("hgrn_g", 8, htmp)
            e.wait_ge(v_full, 1)
            join()
            for b in range(4):
                e.activation(hv[:, b // 2, (b % 2) * 512:(b % 2 + 1) * 512], bank[b][:, :], ACT.Copy)
            join()
            e.activation(hb[:, :, :], hb[:, :, :], ACT.Ln)
            join()
            join()
            for n in range(len(LEVELS)):
                x = (hx, ht)[n % 2]
                e.wait_ge(lvl_diff, n + 1)
                e.activation(x[:, :, :], x[:, :, :], ACT.Exp).then_inc(lvl_exp, 1)
            join()
            e.activation(hx[:, :, :], hb[:, :, :], ACT.Exp)
            e.activation(ebl[:, :], hb[:, :, :].rearrange("p h (c t) -> p (h c) t", c=ST)[:, :, P - 1],
                         ACT.Exp)
            join()
            e.activation(ht[:, :, :], ht[:, :, :], ACT.Exp)
            join()
            join()
            join()
            for hh in range(HEADS):
                e.activation(hb[:, hh, :], bank[hh][:, :], ACT.Copy)
            join()
            for g in range(2):
                join()
                for j in range(4):
                    e.activation(hk[:, 4 * g + j, :], bank[j][:, :], ACT.Copy)
                join()
            e.activation(hx[:, :, :], hk[:, :, :], ACT.Square)
            join()
            for hh in range(HEADS):
                e.wait_ge(og_sum, hh + 1)
                e.activation(hq[:, hh, :], bank[hh][:, :], ACT.Ln, scale=1.0 / P, bias=col("eps"))
            e.drain()
            e.activation(hq[:, :, :], hq[:, :, :], ACT.Exp, scale=-0.5)
            join()
            join()
            split_act(e, split_og)
            join()
            join()

            def mlp(n):
                norm(f"mlp{n}")
                for k in range(2):
                    f = flow[f"mlp{n}_up{k}"]
                    banks_are_free(e, f)

                    def step(m, j):
                        e.wait_ge(f.full, m + 1)
                        e.wait_ge(f.b, m + 1)
                        e.activation(ur[:, j, :], bank[j][:, :], ACT.Relu).then_inc(f.free, 1)
                        e.drain()
                        e.activation(uh[:, m, :], ur[:, j, :], ACT.Square).then_inc(f.a, 1)
                    looped(e, 16, 4, step)
                    join()
                    join()

            mlp(0)
            e.dma_start(rp[:, :, :], rope).then_inc(extra_loaded, 16)
            norm("kv")
            copies("kv", [whole(ckv[:, 0, :]), whole(ckv[:, 1, :]), whole(rt[:, 2, :]), whole(rt[:, 3, :])])
            norm("ckv")
            norm("mla")
            copies("dq", [whole(cq[:, 0, :]), whole(cq[:, 1, :])])
            norm("cq")
            for g in range(4):
                join()
                for j in range(4):
                    e.activation(gk[:, j, :], bank[j][:, :], ACT.Copy)
                join()
                join()
                for t in range(ST):
                    e.activation(gv[:, t, :], bank[2 + t][:, :], ACT.Copy)
                join()
                attention_act(e, mla, g, lambda n: bank[n % 3])
                join()
            split_act(e, split_mo)
            join()
            join()
            mlp(1)
            norm("final")
            norm("mix")
            copies("dsa_in", [
                [(slice(0, P), dsmall[:, :]), (slice(0, 64), dki[0:64, :]), (slice(0, 64), dki[64:P, :])],
                *[whole(dqi[:, j, :]) for j in range(4)], whole(dcraw[:, :])])
            f = flow["dsa_q"]
            banks_are_free(e, f)

            def step(m, j):
                e.wait_ge(f.full, m + 1)
                e.activation(dq2[:, m, :], bank[j][:, :], ACT.Copy, scale=0.125).then_inc(f.free, 1)
            looped(e, 8, 4, step)
            join()
            for dst, src in ((boh, bucket), (rb, rel_bias), (wuk, w_uk2), (wuv, w_uv2)):
                e.dma_start(dst[:], src).then_inc(extra_loaded, 16)
            norm("c2")
            join()
            e.activation(dnat[:, :, :], four(bank[0][:, :]), ACT.Copy)
            e.activation(dcn[:, :, :], four(bank[1][:, :]), ACT.Copy)
            e.activation(drow[:, :], bank[2][0:AHEADS, 0:DISTS], ACT.Copy)
            join()
            e.dma_start(toep_dram, drow[:, :]).then_inc(toep_stored, 16)
            e.wait_ge(toep_stored, 16)
            e.dma_start(tp[:, :, :], bass.AP(tensor=toep_dram.tensor, offset=0,
                                             ap=[[1, P], [DISTS, AHEADS], [1, 2 * P]])
                        ).then_inc(toep_loaded, 16)
            for n in range(24):
                e.wait_ge(ix_full, n + 1)
                if n >= 4:
                    e.wait_ge(ix_used, n - 3)
                wd = (n // 8 + 2) * P
                e.activation(dre[:, n % 4, 0:wd], bank[n % 4][:, 0:wd], ACT.Relu).then_inc(ix_relu, 1)
            e.wait_ge(flip_full, 1)
            for b in range(8):
                e.activation(tp[:, 2 * b:2 * b + 2, :].rearrange("p h j -> p (h j)"), bank[b][:, :], ACT.Copy)
            join()
            for g in range(4):
                join()
                for j in range(4):
                    e.activation(dql[:, j, :], bank[j][:, :], ACT.Copy)
                join()
                attention_act(e, dsa, g, lambda n: lg2[:, n % 2, :])
                join()
                join()
                for j in range(2):
                    e.activation(dq2[:, 2 * g + j, :], bank[j][:, :], ACT.Copy)
                join()
            split_act(e, split_att)
            join()
            f = flow["att_out"]
            banks_are_free(e, f)

            def step_att(m, j):
                e.wait_ge(f.full, m + 1)
                e.activation(mg[:, m, :], bank[j][:, :], ACT.Copy).then_inc(f.free, 1)
            looped(e, 8, 4, step_att)
            join()
            gate("g_att", 8, gsig)

            fx = flow["xbc"]
            banks_are_free(e, fx)

            def step_conv(m, j):
                e.wait_ge(fx.full, m + 1)
                e.wait_ge(fx.b, m + 1)
                e.activation(cu[:, j % 2, 3:3 + S], bank[j][:, :], ACT.Copy).then_inc(fx.free, 1)
                e.wait_ge(fx.b, m + 3)
                e.activation(cs[:, j % 2, :], ca[:, j, :], ACT.Sigmoid).then_inc(fx.a, 1)
            looped(e, 24, 4, step_conv)
            join()
            join()
            e.activation(sz[:, 2, :], sz[:, 1, :], ACT.Exp)
            e.activation(sam[:, :], col("a_log", 0, 32), ACT.Exp)
            join()
            join()
            join()
            e.activation(sact[:, :], bank[2][0:32, :], ACT.Copy)
            join()
            e.activation(scd[:, :, :], sat[:, :, :], ACT.Exp)
            e.activation(sds[:, :, :], sds[:, :, :], ACT.Exp)
            join()
            for g in range(4):
                join()
                e.activation(sbn[:, :, :], four(bank[4][:, :]), ACT.Copy)
                join()
                join()
                for p in range(4):
                    n = 4 * g + p
                    if p:
                        e.wait_ge(sg_yd, n)
                    e.wait_ge(sg_sel, n + 1)
                    e.activation(sea[:, :], bank[2][:, :], ACT.Exp).then_inc(sg_exp, 1)
                    for q in range(2):
                        e.wait_ge(sg_sub, 2 * n + q + 1)
                        e.activation(sgt[:, q, :], sgt[:, q, :], ACT.Exp).then_inc(sg_exp, 1)
                join()
            gate("z", 16, zt)
            f2 = flow["g_ssm"]
            banks_are_free(e, f2)

            def step_gss(m, j):
                e.wait_ge(f2.full, m + 1)
                e.activation(gss[:, m, :], bank[j][:, :], ACT.Sigmoid).then_inc(f2.free, 1)
            looped(e, 8, 4, step_gss)
            join()
            for g in range(4):
                norm_act(e, norms_y[g])
                join()
            split_act(e, split_y)
            join()
            join()
            split_act(e, split_mg)
            join()
            join()
            norm("ffn")
            ff = flow["ffn_up"]
            banks_are_free(e, ff)

            with e.Fori(0, FT // 2) as i:
                for r in range(2):
                    m, pair = 4 * i + 2 * r, 2 * i + r
                    for k in range(2):
                        e.wait_ge(ff.full, m + (k + 1))
                        e.wait_ge(ff.b, m + (k + 1))
                        e.activation(fu[:, 2:2 + S], bank[2 * r + k][:, :], ACT.Copy).then_inc(ff.free, 1)
                    e.activation(fs[:, :], fa[:, :], ACT.Sigmoid).then_inc(ff.a, 1)
                    e.wait_ge(ff.c, pair + 1)
                    e.activation(fh[:, pair, :], fa[:, :], ACT.Copy).then_inc(ff.a, 1)
            join()
            join()
            norm("last")
            e.dma_start(out, h[:, :, :]).then_inc(stored, 16)
            e.wait_ge(stored, 16)

        @block.vector
        def _(e):
            join = joiner(e, dve_step, (pe_step, act_step))
            tt, ts, stt = e.tensor_tensor, e.tensor_scalar, e.scalar_tensor_tensor
            e.wait_ge(consts_loaded, 32)

            def norm(name):
                norm_dve(e, norms[name])
                join()

            def gated(name, mt, put):
                f = flow[name]
                banks_are_free(e, f)

                def step(m, j):
                    e.wait_ge(f.a, m + 1)
                    put(m, j).then_inc(f.free, 1)
                looped(e, mt, 4, step)
                join()

            def residual(name):
                f = flow[name]
                banks_are_free(e, f)

                def step(m, j):
                    e.wait_ge(f.full, m + 1)
                    tt(h[:, m, :], bank[j][:, :], h[:, m, :], ALU.add).then_inc(f.free, 1)
                looped(e, 8, 4, step)
                join()

            tt(lbt[:, 2, :], col("lb0", 0, 8), col("lb1", 0, 8), ALU.max)
            e.drain()
            tt(lbt[:, 0, :], col("lb0", 0, 8), lbt[:, 2, :], ALU.subtract)
            tt(lbt[:, 1, :], col("lb1", 0, 8), lbt[:, 2, :], ALU.subtract)
            join()
            join()
            tt(lbt[:, 2, :], lbt[:, 0, :], lbt[:, 1, :], ALU.add)
            e.drain()
            e.reciprocal(lbt[:, 1, :], lbt[:, 2, :])
            e.drain()
            tt(lb[:, :], lbt[:, 0, :], lbt[:, 1, :], ALU.mult)
            e.drain()
            ts(oml[:, :], lb[:, :], -1.0, 1.0, ALU.mult, ALU.add)
            norm("hgrn")
            gated("hgrn_q", 8, lambda m, j: tt(hq[:, m, :], bank[j][:, :], htmp[:, j, :], ALU.mult))
            gated("hgrn_f", 8, lambda m, j: ts(hb[:, m, :], htmp[:, j, :], oml[:, bass.ds(m, 1)],
                                               lb[:, bass.ds(m, 1)], ALU.mult, ALU.add))
            gated("hgrn_g", 8, lambda m, j: tt(hg[:, m, :], bank[j][:, :], htmp[:, j, :], ALU.mult))
            e.wait_ge(v_full, 1)
            join()
            for b in range(4, 8):
                e.tensor_copy(hv[:, b // 2, (b % 2) * 512:(b % 2 + 1) * 512], bank[b][:, :])
            ts(hk[:, :, :], hb[:, :, :], -1.0, 1.0, ALU.mult, ALU.add)
            join()
            join()
            for hh in range(HEADS):
                e.tensor_tensor_scan(hb[:, hh, :], col("restart", 0, S), hb[:, hh, :], 0.0, ALU.mult, ALU.add)
            join()

            def level_exponents(n):
                L = LEVELS[n]
                x, b = half((hx, ht)[n % 2], L), half(hb, L)
                mid = b[:, :, 0, L - 1:L].broadcast_to([P, HEADS * S // (2 * L), L])
                tt(x[:, :, 1, :], b[:, :, 1, :], mid, ALU.subtract)
                tt(x[:, :, 0, :], mid, b[:, :, 0, :], ALU.subtract).then_inc(lvl_diff, 1)

            def place_level(n):
                e.wait_ge(lvl_mm, n + 2)
                for hh in range(HEADS):
                    e.copy_predicated(four(hs[:, hh, :]), to_four(col("levels", n * P, P).bitcast(I32)),
                                      four(bank[hh][:, :]))
                e.drain()

            level_exponents(0)
            e.wait_ge(lvl_mm, 1)
            for hh in range(HEADS):
                tt(four(hs[:, hh, :]), four(bank[hh][:, :]), to_four(ident), ALU.mult)
            e.drain()
            for n in range(len(LEVELS)):
                L = LEVELS[n]
                if n:
                    place_level(n - 1)
                if n + 1 < len(LEVELS):
                    level_exponents(n + 1)
                e.wait_ge(lvl_exp, n + 1)
                x = half((hx, ht)[n % 2], L)
                tt(x[:, :, 1, :], x[:, :, 1, :], half(hq, L)[:, :, 1, :], ALU.mult)
                tt(x[:, :, 0, :], x[:, :, 0, :], half(hk, L)[:, :, 0, :], ALU.mult).then_inc(lvl_x, 1)
            place_level(len(LEVELS) - 1)
            join()
            b4 = hb[:, :, :].rearrange("p h (c t) -> p (h c) t", c=ST)
            t4 = ht[:, :, :].rearrange("p h (c t) -> p (h c) t", c=ST)
            tt(t4, b4[:, :, P - 1:P].broadcast_to([P, HEADS * ST, P]), b4, ALU.subtract)
            join()
            tt(hx[:, :, :], hx[:, :, :], hq[:, :, :], ALU.mult)
            join()
            tt(ht[:, :, :], ht[:, :, :], hk[:, :, :], ALU.mult)
            join()
            join()
            join()
            for g in range(2):
                for c in range(ST - 1):
                    for j in range(4):
                        hh = 4 * g + j
                        state, upd = ht[:, hh // 4, chunk(hh % 4)], bank[4 + j][:, chunk(c)]
                        e.wait_ge(st_pe, 12 * g + 4 * c + j + 1)
                        if c == 0:
                            e.tensor_copy(state, upd).then_inc(st_dve, 1)
                        else:
                            stt(state, state, ebl[:, ST * hh + c:ST * hh + c + 1], upd,
                                ALU.mult, ALU.add).then_inc(st_dve, 1)
                join()
                join()
            join()
            join()
            for hh in range(HEADS):
                stt(hk[:, hh, :], hk[:, hh, :], col("g_norm"), hq[:, hh, :], ALU.mult, ALU.mult)
            e.drain()
            tt(hk[:, :, :], hk[:, :, :], hg[:, :, :], ALU.mult)
            join()
            split_dve(e, split_og)
            join()
            residual("hgrn_o")

            def mlp(n):
                norm(f"mlp{n}")
                for k in range(2):
                    f = flow[f"mlp{n}_up{k}"]
                    e.drain().then_inc(f.b, 4)

                    def step(m, j):
                        e.wait_ge(f.free, m + 5)
                        tt(ut[:, j, :], ur[:, j, :], ur[:, j, :], ALU.mult)
                        e.drain()
                        e.wait_ge(f.a, m + 1)
                        tt(ul[:, m, :], ut[:, j, :], uh[:, m, :].bitcast(F32), ALU.subtract).then_inc(f.b, 1)
                    looped(e, 16, 4, step)
                    join()
                    residual(f"mlp{n}_down{k}")

            def rotate(x1, x2, o1, o2):
                tt(rt[:, 0, :], x1, rp[:, 0, :], ALU.mult)
                tt(o1, x2, rp[:, 1, :], ALU.mult)
                e.drain()
                tt(o1, rt[:, 0, :], o1, ALU.subtract)
                tt(rt[:, 1, :], x2, rp[:, 0, :], ALU.mult)
                tt(o2, x1, rp[:, 1, :], ALU.mult)
                e.drain()
                tt(o2, rt[:, 1, :], o2, ALU.add)

            mlp(0)
            norm("kv")
            join()
            e.wait_ge(extra_loaded, 16)
            rotate(rt[:, 2, :], rt[:, 3, :], kr[:, 0, :], kr[:, 1, :])
            norm("ckv")
            norm("mla")
            join()
            norm("cq")
            for g in range(4):
                join()
                for j in range(4):
                    e.tensor_copy(gq[:, j, :], bank[4 + j][:, :])
                join()
                join()
                rotate(bank[0][:, :], bank[1][:, :], gr[:, 0, :], gr[:, 1, :])
                join()
                attention_dve(e, mla, g, lambda e_, n: bank[n % 3], lambda j: mo[:, 4 * g + j, :])
                join()
            split_dve(e, split_mo)
            join()
            residual("mla_o")
            mlp(1)
            norm("final")
            norm("mix")
            join()
            join()
            norm("c2")
            join()
            join()
            for i in range(1, ST):
                wd = (i + 1) * P
                acc = dsc[:, i - 1, 0:wd]
                for j in range(8):
                    n = 8 * (i - 1) + j
                    wcol = dnat[:, i, 64 + j:65 + j]
                    e.wait_ge(ix_relu, n + 1)
                    if j == 0:
                        ts(acc, dre[:, n % 4, 0:wd], wcol, None, ALU.mult).then_inc(ix_used, 1)
                    else:
                        e.drain()
                        stt(acc, dre[:, n % 4, 0:wd], wcol, acc, ALU.mult, ALU.add).then_inc(ix_used, 1)
                e.drain()
                tt(dsc[:, i - 1, chunk(i)], dsc[:, i - 1, chunk(i)], col("neg", 0, P), ALU.add)
            e.drain()
            for t in range(TOPK // 8):
                for i in range(1, ST):
                    e.max(dm8[:, i - 1, :], (dwk if t else dsc)[:, i - 1, 0:(i + 1) * P])
                e.drain()
                for i in range(1, ST):
                    wd = (i + 1) * P
                    e.match_replace(dwk[:, i - 1, 0:wd], dm8[:, i - 1, :], (dwk if t else dsc)[:, i - 1, 0:wd],
                                    TAKEN)
                e.drain()
            e.tensor_copy(dsm[:, 0, 0:P], col("neg", 0, P))
            for i in range(1, ST):
                wd = (i + 1) * P
                ts(dsm[:, i, 0:wd], dwk[:, i - 1, 0:wd], TAKEN / 2, NEG, ALU.is_ge, ALU.mult)
            join()
            for g in range(4):
                join()
                join()

                def logits(e_, n):
                    i = n % 4
                    x = lg2[:, n % 2, :]
                    tt(x[:, 0:(i + 1) * P], bank[n % 3][:, 0:(i + 1) * P], dsm[:, i, 0:(i + 1) * P], ALU.add)
                    e.drain()
                    lo = max(i - 1, 0) * P
                    near = tp[:, 4 * g + n // 4, (P if i == 0 else 0):2 * P]
                    tt(x[:, lo:(i + 1) * P], x[:, lo:(i + 1) * P], near, ALU.add)
                    e.drain()
                    return x

                attention_dve(e, dsa, g, logits, lambda j: dlo[:, j, :])
                join()
                join()
                join()
            split_dve(e, split_att)
            join()
            join()
            gated("g_att", 8, lambda m, j: tt(mg[:, m, :], mg[:, m, :], gsig[:, j, :], ALU.mult))

            def convolve(dst, src, taps, name, nt_, m):
                ts(dst, src[:, 0:S], C[:, bass.ds(COL[name] + m, 1)], C[:, bass.ds(COL[name + "_b"] + m, 1)],
                   ALU.mult, ALU.add)
                for k in range(1, taps):
                    e.drain()
                    last = stt(dst, src[:, k:k + S], C[:, bass.ds(COL[name] + k * nt_ + m, 1)], dst,
                               ALU.mult, ALU.add)
                return last

            fx = flow["xbc"]
            e.memset(cu[:, :, 0:3], 0.0)
            e.drain().then_inc(fx.b, 2)

            def step_conv(m, j):
                e.wait_ge(fx.free, m + 5)
                convolve(ca[:, j, :], cu[:, j % 2, :], 4, "conv_ssm", 24, m).then_inc(fx.b, 1)
                e.wait_ge(fx.a, m + 1)
                tt(xbc[:, m, :], ca[:, j, :], cs[:, j % 2, :], ALU.mult)
            looped(e, 24, 4, step_conv)
            join()

            def z3(k):
                return sz[:, k, :].rearrange("p (c n) -> p c n", n=32)

            tt(z3(0), dnat[:, :, 96:P], col("dt_bias", 0, 32).unsqueeze(1).broadcast_to([P, ST, 32]), ALU.add)
            e.drain()
            stt(sz[:, 1, :], sz[:, 0, :], -1.0, sz[:, 0, :], ALU.mult, ALU.min)
            join()
            join()
            z0, z1, z2, z4, z5 = (sz[:, k, :] for k in (0, 1, 2, 4, 5))
            ts(z1, z2, 2.0, None, ALU.add)
            e.drain()
            e.reciprocal(z5, z1)
            e.drain()
            tt(z4, z2, z5, ALU.mult)
            e.drain()
            tt(z1, z4, z4, ALU.mult)
            e.drain()
            ts(z5, z1, 1.0 / 15, 1.0 / 13, ALU.mult, ALU.add)
            for k in (11, 9, 7, 5, 3, 1):
                e.drain()
                tt(z5, z5, z1, ALU.mult)
                e.drain()
                ts(z5, z5, 1.0 / k, None, ALU.add)
            e.drain()
            tt(z5, z5, z4, ALU.mult)
            e.drain()
            ts(z5, z5, 2.0, None, ALU.mult)
            ts(z0, z0, 0.0, None, ALU.max)
            e.drain()
            tt(sdt[:, :, :], z3(5), z3(0), ALU.add)
            e.drain()
            stt(sad[:, :, :], sdt[:, :, :], -1.0, sam[:, :].unsqueeze(1).broadcast_to([P, ST, 32]),
                ALU.mult, ALU.mult)
            join()
            join()
            e.tensor_copy(sac[:, :, :], bank[0][:, 0:P].rearrange("p (c n) -> p c n", n=32))
            e.tensor_copy(sat[:, :, :], bank[1][:, 0:P].rearrange("p (c n) -> p c n", n=32))
            e.drain()
            tt(sds[:, :, :], sat[:, :, :], sac[:, :, :], ALU.subtract)
            join()
            join()
            for g in range(4):
                g8 = slice(8 * g, 8 * g + 8)

                def by_head(x):
                    return x.rearrange("p (n d) -> p n d", d=64)

                join()
                for c in range(ST):
                    tt(by_head(sxn[:, c, :]), by_head(bank[c][:, :]), heads_out(sdt[:, c, g8], 8), ALU.mult)
                tt(scb[:, :, :], four(bank[5][:, :]), to_four(col("tri", 0, P)), ALU.mult)
                join()
                for c in range(ST - 1):
                    n = 24 + 3 * g + c
                    if c:
                        e.drain()
                    tt(by_head(sxd[:, :]), by_head(sxn[:, c, :]), heads_out(sds[:, c, g8], 8),
                       ALU.mult).then_inc(st_dve, 1)
                    if c:
                        tt(by_head(sst[:, c, :]), by_head(sst[:, c - 1, :]), heads_out(scd[:, c, g8], 8), ALU.mult)
                        e.drain()
                    e.wait_ge(st_pe, n + 1)
                    if c:
                        tt(sst[:, c, :], sst[:, c, :], bank[c][:, :], ALU.add)
                    else:
                        e.tensor_copy(sst[:, 0, :], bank[0][:, :])
                join()
                for p in range(4):
                    n = 4 * g + p
                    hh = 8 * g + 2 * p
                    t = 4 * g + p
                    e.wait_ge(sg_sel, n + 1)
                    for q in range(2):
                        tt(four(sgt[:, q, :]), four(bank[q][:, :]),
                           sac[:, :, hh + q:hh + q + 1].broadcast_to([P, ST, P]), ALU.subtract)
                        e.drain()
                        ts(sgt[:, q, :], sgt[:, q, :], 0.0, None, ALU.min).then_inc(sg_sub, 1)
                    e.wait_ge(sg_exp, 3 * n + 3)
                    e.drain()
                    for q in range(2):
                        mm = tt(sgt[:, q, :], sgt[:, q, :], scb[:, :, :].rearrange("p c t -> p (c t)"), ALU.mult)
                    mm.then_inc(sg_g, 1)
                    e.wait_ge(sg_y, n + 1)
                    tt(sea[:, P:S], bank[5][:, P:S], sea[:, P:S], ALU.mult)
                    stt(xbc[:, t, :], xbc[:, t, :], col("d_skip", t), bank[4][:, :], ALU.mult, ALU.add)
                    e.drain()
                    tt(xbc[:, t, P:S], xbc[:, t, P:S], sea[:, P:S], ALU.add).then_inc(sg_yd, 1)
                join()

            def put_z(m, j):
                tt(zt[:, j, :], bank[j][:, :], zt[:, j, :], ALU.mult)
                e.drain()
                return tt(xbc[:, m, :], xbc[:, m, :], zt[:, j, :], ALU.mult)

            gated("z", 16, put_z)
            join()
            for g in range(4):
                norm_dve(e, norms_y[g])
                join()
            split_dve(e, split_y)
            join()
            fo = flow["ssm_out"]
            banks_are_free(e, fo)

            def step_out(m, j):
                e.wait_ge(fo.full, m + 1)
                tt(sq[:, j, :], bank[j][:, :], gss[:, m, :], ALU.mult)
                e.drain()
                tt(mg[:, m, :], mg[:, m, :], sq[:, j, :], ALU.add).then_inc(fo.free, 1)
            looped(e, 8, 4, step_out)
            join()
            split_dve(e, split_mg)
            join()
            residual("w_out")
            norm("ffn")
            ff = flow["ffn_up"]
            e.memset(fu[:, 0:2], 0.0)
            e.drain().then_inc(ff.b, 1)
            with e.Fori(0, FT // 2) as i:
                for r in range(2):
                    m, pair = 4 * i + 2 * r, 2 * i + r
                    e.wait_ge(ff.free, m + 5)
                    convolve(fa[:, :], fu, 3, "conv_ffn", 44, m).then_inc(ff.b, 1)
                    e.wait_ge(ff.free, m + 6)
                    convolve(fv[:, :], fu, 3, "conv_ffn", 44, m + 1).then_inc(ff.b, 1)
                    e.wait_ge(ff.a, 2 * pair + 1)
                    tt(fa[:, :], fa[:, :], fs[:, :], ALU.mult)
                    e.drain()
                    tt(fa[:, :], fa[:, :], fv[:, :], ALU.mult).then_inc(ff.c, 1)
                    e.wait_ge(ff.a, 2 * pair + 2)
                    tt(fl[:, pair, :], fa[:, :], fh[:, pair, :].bitcast(F32), ALU.subtract)
                    e.drain()
            join()
            residual("ffn_down")
            norm("last")


def blocks(w):
    k, m = w.shape[0] // P, w.shape[1] // P
    return w.reshape(k, P, m, P).transpose(2, 0, 1, 3).reshape(k * m, P, P)


def row_blocks(w):
    k, m = w.shape[0] // P, w.shape[1] // P
    return w.reshape(k, P, m, P).transpose(0, 2, 1, 3).reshape(k * m, P, P)


def weight_stream(a):
    out = []
    for n in ("hgrn_w_q", "hgrn_w_f", "hgrn_w_g"):
        out.append(blocks(a[n][0]))
    out += [row_blocks(a["hgrn_w_i"][0]), blocks(a["hgrn_w_o"][0])]

    def mlp(n):
        up, down = a["mlp_w_up"][n], a["mlp_w_down"][n]
        hf = D_FF // 2
        for k in range(2):
            out.extend([blocks(up[:, k * hf:(k + 1) * hf]), blocks(down[k * hf:(k + 1) * hf])])

    mlp(0)
    dkv = a["kv_w_dkv"]
    out.append(blocks(np.concatenate([dkv[:, :256]] + [dkv[:, 256:288]] * 4 + [dkv[:, 288:320]] * 4, 1)))
    out.append(blocks(a["mla_w_dq"][0]))
    uq = a["mla_w_uq"][0].reshape(256, 16, 192)
    uk, uv = a["kv_w_uk"], a["kv_w_uv"]
    for g in range(4):
        hs = slice(4 * g, 4 * g + 4)
        out.append(blocks(uk[:, 512 * g:512 * (g + 1)]))
        out.append(blocks(uq[:, hs, :128].reshape(256, 512)))
        out.append(blocks(np.concatenate([uq[:, hs, 128:160].reshape(256, 128),
                                          uq[:, hs, 160:192].reshape(256, 128)], 1)))
        out.append(np.zeros((4, P, P), uk.dtype))
        out.append(row_blocks(uv[:, 512 * g:512 * (g + 1)]))
    out.append(blocks(a["mla_w_o"][0]))
    mlp(1)
    w = a["w_in_2"][0]
    q, c, qi, ki, wi, z, xbc, dt, ga, gs = np.split(w, np.cumsum([1024, 128, 512, 64, 8, 2048, 3072, 32, 1024]), 1)
    small = np.concatenate([ki, wi, np.zeros((D, 24), w.dtype), dt], 1)
    out += [blocks(small), blocks(qi), blocks(c), blocks(q), blocks(a["w_att_out_2"][0]), blocks(ga),
            blocks(xbc), blocks(z), blocks(gs), blocks(a["w_ssm_out_2"][0]), blocks(a["w_out_2"][0])]
    up = a["w_ffn_up_2"][0].reshape(D, 2, FT, P).transpose(0, 2, 1, 3).reshape(D, 2 * FFN)
    out += [blocks(up), blocks(a["w_ffn_down_2"][0])]
    s = np.concatenate(out)
    s = np.concatenate([s, np.zeros((TILES * BLK - s.shape[0], P, P), s.dtype)])
    return np.ascontiguousarray(s.reshape(TILES, BLK, P, P).transpose(0, 2, 1, 3)).reshape(TILES, P, BLK * P)


def columns(a):
    c = np.zeros((P, NCOLS), np.float32)

    def put(name, x, rows=P):
        c[:rows, COL[name]:COL[name] + x.shape[1]] = x

    i = np.arange(P)
    put("ident", np.eye(P, dtype=np.float32))
    put("ones", np.ones((P, P), np.float32))
    put("neg", np.where(i[None, :] > i[:, None], NEG, 0.0).astype(np.float32))
    put("tri", (i[:, None] <= i[None, :]).astype(np.float32))
    put("flip", np.ascontiguousarray(np.eye(P, dtype=np.float32)[::-1]))
    put("restart", np.tile((np.arange(S) % P != 0).astype(np.float32), (P, 1)))
    for n, L in enumerate(LEVELS):
        same = i[:, None] // (2 * L) == i[None, :] // (2 * L)
        put_at = COL["levels"] + n * P
        c[:, put_at:put_at + P] = same & (i[:, None] % (2 * L) < L) & (i[None, :] % (2 * L) >= L)
    put("eps", np.full((P, 1), EPS, np.float32))

    def feat(x):
        return x.reshape(-1, P).T

    for name, x in (("hgrn_norm", a["hgrn_norm"][0]), ("mla_norm", a["mla_norm"][0]),
                    ("kv_in_norm", a["kv_in_norm"]), ("mlp_norm0", a["mlp_norm"][0]),
                    ("mlp_norm1", a["mlp_norm"][1]), ("final_norm", a["final_norm"]),
                    ("norm_mix", a["norm_mix_2"][0]), ("norm_ffn", a["norm_ffn_2"][0]),
                    ("norm_final", a["norm_final_2"]), ("g_norm", a["hgrn_g_norm"][0]),
                    ("lb0", a["hgrn_lb_logits"][0]), ("lb1", a["hgrn_lb_logits"][1]),
                    ("q_norm", a["mla_q_norm"][0]), ("kv_norm", a["kv_norm"]),
                    ("kv_norm2", a["kv_norm_2"][0]), ("ssm_norm", a["ssm_norm_2"][0]),
                    ("conv_ssm_b", a["conv_ssm_b_2"][0]),
                    ("d_skip", np.repeat(a["d_skip_2"][0], 64))):
        put(name, feat(x))
    put("dt_bias", np.tile(a["dt_bias_2"][0], (P, 1)))
    put("a_log", np.tile(a["a_log_2"][0], (P, 1)))
    put("conv_ssm", feat(a["conv_ssm_w_2"][0].reshape(-1)))

    def pairs(x):
        return x.reshape(-1, 2, FT, P).transpose(0, 2, 1, 3).reshape(-1)

    put("conv_ffn", feat(pairs(a["conv_ffn_w_2"][0])))
    put("conv_ffn_b", feat(pairs(a["conv_ffn_b_2"][0])))
    return c


def rope_rows():
    f = (np.float32(10000.0) ** (-np.arange(32, dtype=np.float32) / np.float32(32))).astype(np.float32)
    ang = np.arange(S, dtype=np.float32)[None, :] * f[:, None]
    return np.tile(np.stack([np.cos(ang), np.sin(ang)], 1).astype(np.float32), (4, 1, 1))


def bucket_rows():
    dist = np.maximum(255 - np.arange(DISTS), 0)
    large = 16 + (np.log(np.maximum(dist, 1).astype(np.float32) / np.float32(16)).astype(np.float32)
                  / np.float32(np.log(8.0)) * np.float32(16)).astype(np.int32)
    b = np.where(dist < 16, dist, np.minimum(large, 31))
    one = (np.arange(BUCKETS)[:, None] == b[None, :]).astype(np.float32)
    one[31] -= 1.0
    return one


def kernel(**inputs):
    import concourse.bacc as bacc
    from concourse.bass_utils import run_bass_kernel_spmd

    a = {k: np.asarray(v) for k, v in inputs.items()}
    arrays = {
        "stream": weight_stream(a),
        "cols": columns(a),
        "rope": rope_rows(),
        "bucket": bucket_rows(),
        "w_uk2": np.ascontiguousarray(a["w_uk_2"][0].reshape(8, P, P).transpose(1, 0, 2)),
        "w_uv2": np.ascontiguousarray(a["w_uv_2"][0].transpose(2, 0, 1)),
        "x_in": np.ascontiguousarray(a["x"][0].reshape(S, KT, P).transpose(2, 1, 0)),
        "rel_bias": np.ascontiguousarray(a["rel_bias_2"]),
    }
    nc = bacc.Bacc("TRN2", target_bir_lowering=False, num_devices=1)
    args = [nc.dram_tensor(n, x.shape, F32, kind="ExternalInput").ap() for n, x in arrays.items()]
    toep = nc.dram_tensor("bias_by_distance", (AHEADS, DISTS), F32, kind="Internal").ap()
    out = nc.dram_tensor("out", (P, KT, S), F32, kind="ExternalOutput").ap()
    build(nc, *args, toep, out)
    r = run_bass_kernel_spmd(nc, [arrays], core_ids=[0])
    got = r.results[0]["out"]
    return np.ascontiguousarray(got.transpose(2, 1, 0)).reshape(1, S, D)
```

```python
from contextlib import ExitStack

import numpy as np
import concourse.bass as bass
from concourse import mybir
from concourse.alu_op_type import AluOpType as ALU

ACT = mybir.ActivationFunctionType
AX = mybir.AxisListType
F32 = mybir.dt.float32
F32R = mybir.dt.float32r
I32 = mybir.dt.int32

P = 128
D = 1024
S = 512
KT = D // P
ST = S // P
EPS = 1e-6
NEG = -1e30
TAKEN = -3e38
HEADS = 8
LEVELS = [64, 32, 16, 8, 4, 2, 1]
AHEADS = 16
MLA_SCALE = float(192) ** -0.5
D_FF = 4096
FFN = 2816
FT = FFN // P
TOPK = 128
SLOTS = 4
LOOK = SLOTS - 1
BLK = 8

STREAM = [
    ("hgrn_q", 64), ("hgrn_f", 64), ("hgrn_g", 64), ("hgrn_i", 64), ("hgrn_o", 64),
    ("mlp0_up0", 128), ("mlp0_down0", 128), ("mlp0_up1", 128), ("mlp0_down1", 128),
    ("kv", 32), ("dq", 16), ("mla", 4 * 32), ("mla_o", 128),
    ("mlp1_up0", 128), ("mlp1_down0", 128), ("mlp1_up1", 128), ("mlp1_down1", 128),
    ("dsa_in", 6 * 8), ("dsa_q", 64), ("att_out", 64), ("g_att", 64), ("xbc", 24 * 8), ("z", 128),
    ("g_ssm", 64), ("ssm_out", 128), ("w_out", 64), ("ffn_up", 2 * FT * 8), ("ffn_down", FT * 8),
]
TILES = -(-sum(n for _, n in STREAM) // (BLK * SLOTS)) * SLOTS

COLS = [
    ("ident", P), ("ones", P), ("neg", P), ("tri", P), ("flip", P), ("restart", S), ("levels", len(LEVELS) * P),
    ("hgrn_norm", 8), ("mla_norm", 8), ("kv_in_norm", 8), ("mlp_norm0", 8), ("mlp_norm1", 8),
    ("final_norm", 8), ("norm_mix", 8), ("norm_ffn", 8), ("norm_final", 8), ("g_norm", 1),
    ("lb0", 8), ("lb1", 8), ("q_norm", 2), ("kv_norm", 2), ("kv_norm2", 1), ("dt_bias", 32),
    ("a_log", 32), ("d_skip", 16), ("ssm_norm", 16), ("conv_ssm", 4 * 24), ("conv_ssm_b", 24),
    ("conv_ffn", 3 * 44), ("conv_ffn_b", 44), ("eps", 1),
]
COL = {}
NCOLS = 0
for _n, _w in COLS:
    COL[_n] = NCOLS
    NCOLS += _w
BUCKETS = 32
DISTS = 3 * P


def build(nc, stream, cols, rope, bucket, w_uk2, w_uv2, x_in, rel_bias, toep_dram, out):
    ctx = ExitStack()
    with ctx:
        BASE = 16512

        def at(name, kb, shape, dt=F32):
            return nc.alloc_sbuf_tensor_at(name, shape, dt, offset=BASE + int(kb * 1024))

        def sem(name):
            return ctx.enter_context(nc.semaphore(name))

        bank = [ctx.enter_context(nc.psum_tensor(f"bank{i}", [P, 512], F32)) for i in range(8)]

        C = at("consts", 0, [P, NCOLS])
        identr, negr = at("ident_r", 206, [P, P], F32R), at("neg_r", 206.5, [P, P], F32R)
        raw = at("w_raw", 12, [P, SLOTS, BLK * P])
        whi = at("w_hi", 28, [P, SLOTS, BLK * P], F32R)
        wlo = at("w_lo", 44, [P, SLOTS, BLK * P], F32R)
        h = at("residual", 60, [P, KT, S])
        xh = at("x_hi", 76, [P, KT, S], F32R)
        xl = at("x_lo", 92, [P, KT, S], F32R)
        sq = at("squares", 108, [P, KT, S])
        rstd = at("rstd", 124, [P, S])
        nt = at("normed", 126, [P, 4, S])
        hsq, sqsum = at("h_squares", 196, [P, 4, S]), at("square_sum", 204, [P, S])

        def col(name, j=0, n=1):
            return C[:, COL[name] + j:COL[name] + j + n]

        ident, ones = col("ident", 0, P), col("ones", 0, P)

        raw_loaded = [sem(f"raw_loaded{s}") for s in range(SLOTS)]
        hi_ready = [sem(f"hi_ready{s}") for s in range(SLOTS)]
        lo_ready = sem("lo_ready")
        slots_free = sem("slots_free")
        pe_step, act_step, dve_step = sem("pe_step"), sem("act_step"), sem("dve_step")
        consts_loaded, extra_loaded, stored = sem("consts_loaded"), sem("extra_loaded"), sem("stored")
        toep_stored, toep_loaded = sem("toep_stored"), sem("toep_loaded")

        def joiner(e, mine, others):
            steps = [0]

            def join():
                steps[0] += 1
                e.drain().then_inc(mine, 1)
                for o in others:
                    e.wait_ge(o, steps[0])
            return join

        block = ctx.enter_context(nc.Block())

        class Flow:

            def __init__(self, name, more=""):
                self.full = sem(name + "_full")
                self.free = sem(name + "_free")
                self.a = sem(name + "_act") if "a" in more else None
                self.b = sem(name + "_dve") if "b" in more else None
                self.c = sem(name + "_gated") if "c" in more else None

        class Norm:

            def __init__(self, src, gain, oh=None, ol=None, o32=None, rstd=rstd, summed=False,
                         known=False):
                self.rs, self.summed, self.known = rstd, summed, known
                self.src, self.gain, self.oh, self.ol, self.o32 = src, gain, oh, ol, o32
                self.tiles0, self.split0, self.norm0 = norm_counts
                norm_counts[0] += 0 if summed or known else len(src)
                norm_counts[1] += len(src) if oh else 0
                norm_counts[2] += 0 if known else 1
                self.lo = norm_lo

        norm_counts = [0, 0, 0]
        norm_sq, norm_sum, norm_rstd = sem("norm_squares"), sem("norm_sum"), sem("norm_rstd")
        norm_tile, norm_hi, norm_lo = sem("norm_tile"), sem("norm_hi"), sem("norm_lo")

        def tiles(t, n, first=0):
            return [t[:, first + j, :] for j in range(n)]

        def gains(name, n):
            return [col(name, j) for j in range(n)]

        def norm_pe(e, n):
            k = len(n.src)
            if n.known:
                return
            if n.summed:
                e.matmul(bank[7][:, :], ones, sqsum[:, :], start=True, stop=True).then_inc(norm_sum, 1)
                return
            for j in range(k):
                e.wait_ge(norm_sq, n.tiles0 + j + 1)
                mm = e.matmul(bank[7][:, :], ones, sq[:, j, :], start=j == 0, stop=j == k - 1)
            mm.then_inc(norm_sum, 1)

        def norm_act(e, n):
            k = len(n.src)
            if not n.known:
                if not n.summed:
                    for j in range(k):
                        e.activation(sq[:, j, :], n.src[j], ACT.Square).then_inc(norm_sq, 1)
                e.wait_ge(norm_sum, n.norm0 + 1)
                e.activation(n.rs[:, :], bank[7][:, :], ACT.Ln, scale=1.0 / (k * P), bias=col("eps"))
                e.drain()
                e.activation(n.rs[:, :], n.rs[:, :], ACT.Exp, scale=-0.5).then_inc(norm_rstd, 1)
            if n.oh is not None:
                for j in range(k):
                    e.wait_ge(norm_tile, n.split0 + j + 1)
                    e.activation(n.oh[j], nt[:, j % 4, :], ACT.Copy).then_inc(norm_hi, 1)

        def norm_dve(e, n):
            k = len(n.src)
            if not n.known:
                e.wait_ge(norm_rstd, n.norm0 + 1)
            if n.oh is None:
                for j in range(k):
                    e.scalar_tensor_tensor(n.o32[j], n.src[j], n.gain[j], n.rs[:, :], ALU.mult, ALU.mult)
                return

            def low(j):
                e.wait_ge(norm_hi, n.split0 + j + 1)
                e.tensor_tensor(n.ol[j], nt[:, j % 4, :], n.oh[j].bitcast(F32),
                                ALU.subtract).then_inc(norm_lo, 1)

            for j in range(k):
                e.scalar_tensor_tensor(nt[:, j % 4, :], n.src[j], n.gain[j], n.rs[:, :],
                                       ALU.mult, ALU.mult).then_inc(norm_tile, 1)
                if j >= 1:
                    low(j - 1)
            low(k - 1)

        class Split:

            def __init__(self, name, src, oh, ol):
                self.src, self.oh, self.ol = src, oh, ol
                self.hi, self.lo, self.split0 = sem(name + "_hi"), sem(name + "_lo"), 0

        def split_act(e, s):
            for src, oh in zip(s.src, s.oh):
                e.activation(oh, src, ACT.Copy).then_inc(s.hi, 1)

        def split_dve(e, s):
            for j, (src, oh, ol) in enumerate(zip(s.src, s.oh, s.ol)):
                e.wait_ge(s.hi, j + 1)
                e.tensor_tensor(ol, src, oh.bitcast(F32), ALU.subtract).then_inc(s.lo, 1)

        hq, hk = at("hgrn_q", 108, [P, HEADS, S]), at("hgrn_k", 124, [P, HEADS, S])
        hb, hv = at("hgrn_logf", 140, [P, HEADS, S]), at("hgrn_v", 156, [P, ST, D])
        hg, ht = at("hgrn_gate", 172, [P, HEADS, S]), at("hgrn_t", 188, [P, HEADS, S])
        hx, hs = at("hgrn_x", 76, [P, HEADS, S]), at("hgrn_scores", 92, [P, HEADS, S])
        htmp = at("hgrn_tmp", 188, [P, 4, S])
        lb, oml = at("hgrn_lb", 204, [P, 8]), at("hgrn_oml", 204.25, [P, 8])
        lbt = at("hgrn_lbt", 204.5, [P, 3, 8])
        ebl = at("hgrn_ebl", 205, [P, HEADS * ST])

        HH = D_FF // P // 2
        uh, ul = at("hidden_hi", 108, [P, HH, S], F32R), at("hidden_lo", 140, [P, HH, S], F32R)
        ur, ut = at("relu", 172, [P, 4, S]), at("relu_sq", 180, [P, 4, S])

        ckv, cq = at("mla_ckv", 134, [P, 2, S]), at("mla_cq", 138, [P, 2, S])
        ckh, ckl = at("mla_ckv_hi", 142, [P, 2, S], F32R), at("mla_ckv_lo", 146, [P, 2, S], F32R)
        cqh, cql = at("mla_cq_hi", 150, [P, 2, S], F32R), at("mla_cq_lo", 154, [P, 2, S], F32R)
        kr, rp = at("mla_k_rope", 158, [P, S]), at("rope_table", 162, [P, 2, S])
        rt = at("rope_tmp", 166, [P, 4, S])
        mo = at("mla_o", 174, [P, AHEADS, S])
        rstd2 = at("rstd_kv", 174, [P, S])
        gk, gq = at("mla_gk", 76, [P, 4, S]), at("mla_gq", 84, [P, 4, S])
        gr, gv = at("mla_gq_rope", 92, [P, 2, S]), at("mla_gv", 96, [P, ST, 4 * P])
        moh, mol = at("mla_o_hi", 76, [P, AHEADS, S], F32R), at("mla_o_lo", 108, [P, AHEADS, S], F32R)
        pr, pt = at("probs", 104, [P, 3, S]), at("probs_t", 110, [P, ST, S])
        mx, nm = at("row_max", 122, [P, 64]), at("neg_max", 122.25, [P, 64])
        rs, ri = at("row_sum", 122.5, [P, 64]), at("row_inv", 122.75, [P, 64])

        AOFF = 28
        pr2, pt2 = at("probs2", 104 + AOFF, [P, 3, S]), at("probs_t2", 110 + AOFF, [P, ST, S])
        tgh, tgl = at("toeplitz_hi", 124, [P, 4, 2 * P], F32R), at("toeplitz_lo", 128, [P, 4, 2 * P], F32R)
        mx2, nm2 = at("row_max2", 122 + AOFF, [P, 64]), at("neg_max2", 122.25 + AOFF, [P, 64])
        rs2, ri2 = at("row_sum2", 122.5 + AOFF, [P, 64]), at("row_inv2", 122.75 + AOFF, [P, 64])
        dq2 = at("dsa_q", 151, [P, 8, S])
        dql, dlo = at("dsa_qlat", 167, [P, 4, S]), at("dsa_lat", 175, [P, 4, S])
        dc, dcn = at("dsa_c", 183, [P, S]), at("dsa_c_nat", 185, [P, ST, P])
        dsm = at("dsa_selected", 187, [P, ST, S], F32R)
        tp = at("toeplitz", 108, [P, AHEADS, 2 * P])
        dnat = at("small_nat", 204, [P, ST, P])
        dqi, dki = at("dsa_qidx", 132, [P, 4, S]), at("dsa_kidx", 140, [P, S])
        dsmall, dcraw = at("dsa_small", 142, [P, S]), at("dsa_craw", 144, [P, S])
        dre = at("dsa_relu", 167, [P, 4, S])
        dsc, dwk = at("dsa_score", 175, [P, 3, S]), at("dsa_work", 126, [P, 3, S])
        dm8 = at("dsa_max8", 181, [P, 3, 8])
        drow = at("dsa_bias_row", 181.25, [AHEADS, DISTS])
        wuk, wuv = at("dsa_wuk", 195, [P, 8, P]), at("dsa_wuv", 199, [P, AHEADS, 64])
        boh, rb = at("bucket_onehot", 146, [BUCKETS, DISTS]), at("rel_bias", 147.5, [BUCKETS, AHEADS])
        ath, atl = at("att_hi", 108, [P, 8, S], F32R), at("att_lo", 124, [P, 8, S], F32R)
        mg = at("merged", 188, [P, 8, S])
        gsig = at("gate_sig", 140, [P, 4, S])

        xbc = at("ssm_xbc", 108, [P, 24, S])
        xs = xbc
        cu, ca = at("conv_in", 156, [P, 2, S + 4]), at("conv_acc", 160.25, [P, 4, S])
        cs = at("conv_sig", 168.25, [P, 2, S])
        sdt, sad = at("ssm_dt", 156, [P, ST, 32]), at("ssm_adt", 156.5, [P, ST, 32])
        sac, sat = at("ssm_acum", 157, [P, ST, 32]), at("ssm_atot", 157.5, [P, ST, 32])
        sds, scd = at("ssm_decay_states", 158, [P, ST, 32]), at("ssm_chunk_decay", 158.5, [P, ST, 32])
        sam = at("ssm_a", 159, [P, 32])
        sah, sal = at("ssm_acum_t_hi", 159.25, [32, S], F32R), at("ssm_acum_t_lo", 204, [32, S], F32R)
        sxn, sbn = at("ssm_x_nat", 161.25, [P, ST, S]), at("ssm_b_nat", 169.25, [P, ST, P])
        scb = at("ssm_cb", 171.25, [P, ST, P])
        sgt = [[at("ssm_g00", 173.25, [P, S]), at("ssm_g01", 175.25, [P, S])],
               [at("ssm_g10", 183.25, [P, S]), at("ssm_g11", 169.25, [P, S])]]
        sst, sxd = at("ssm_state", 177.25, [P, 3, S]), at("ssm_xd", 183.25, [P, S])
        sz = at("ssm_softplus", 177.25, [P, 6, P])
        sea = [at("ssm_exp_a0", 185.25, [P, S]), at("ssm_exp_a1", 10, [P, S])]
        gss = at("gate_ssm", 140, [P, 8, S])
        zt = at("z_tmp", 156, [P, 4, S])
        zsum, zsq = at("y_square_sum", 164, [P, 4, S]), at("y_squares", 172, [P, 4, S])
        grs = at("y_rstd", 180, [P, 4, S])
        yh, yl = at("y_hi", 76, [P, 16, S], F32R), at("y_lo", 156, [P, 16, S], F32R)

        fh, fl = at("ffn_hi", 108, [P, FT, S], F32R), at("ffn_lo", 152, [P, FT, S], F32R)
        fu, fa = at("ffn_in", 196, [P, S + 4]), at("ffn_gate", 198.25, [P, S])
        fv, fs = at("ffn_val", 200.25, [P, S]), at("ffn_sig", 202.25, [P, S])

        @block.sync
        def _(e):
            e.dma_start(C[:, :], cols).then_inc(consts_loaded, 16)
            e.dma_start(h[:, :, :], x_in).then_inc(consts_loaded, 16)
            for s in range(SLOTS):
                e.dma_start(raw[:, s, :], stream[s]).then_inc(raw_loaded[s], 16)
            with e.Fori(1, TILES // SLOTS) as i:
                for s in range(SLOTS):
                    e.wait_ge(lo_ready, SLOTS * i + (s + 1 - SLOTS))
                    e.dma_start(raw[:, s, :], stream[SLOTS * i + s]).then_inc(raw_loaded[s], 16)

        @block.gpsimd
        def _(e):
            def may_cast(s, turn, tile):
                e.wait_ge(raw_loaded[s], 16 * turn + 16)
                e.wait_ge(slots_free, tile + 1)

            def cast(s):
                e.dma_start(whi[:, s, :], raw[:, s, :]).then_inc(hi_ready[s], 16)

            def low(s, turn):
                e.wait_ge(hi_ready[s], 16 * turn + 16)
                e.tensor_tensor(wlo[:, s, :], raw[:, s, :], whi[:, s, :].bitcast(F32),
                                ALU.subtract).then_inc(lo_ready, 1)

            for s in range(2):
                may_cast(s, 0, s)
                cast(s)
            last = TILES // SLOTS - 1
            with e.Fori(0, last) as i:
                for s in range(SLOTS):
                    n = (s + 2) % SLOTS
                    may_cast(n, i + (s + 2) // SLOTS, SLOTS * i + (s + 2))
                    low(s, i)
                    cast(n)
            for s in range(SLOTS):
                if s < 2:
                    may_cast(s + 2, last, SLOTS * last + s + 2)
                low(s, last)
                if s < 2:
                    cast(s + 2)

        flow = {n: Flow(n, more) for n, more in (
            ("hgrn_q", "a"), ("hgrn_f", "a"), ("hgrn_g", "a"), ("hgrn_o", "a"), ("mlp0_up0", "ab"),
            ("mlp0_down0", ""), ("mlp0_up1", "ab"), ("mlp0_down1", "a"), ("kv", ""), ("dq", ""),
            ("mla_o", "a"), ("mlp1_up0", "ab"), ("mlp1_down0", ""), ("mlp1_up1", "ab"),
            ("mlp1_down1", "a"), ("dsa_in", ""), ("dsa_q", ""), ("att_out", ""), ("g_att", "a"),
            ("xbc", "ab"), ("z", "ab"), ("g_ssm", ""), ("ssm_out", ""), ("w_out", "a"),
            ("ffn_up", "abc"), ("ffn_down", "a"))}

        def weight_reader(e):
            pos = [0]

            class Reader:
                fresh = False

                def block(self, i=None, stride=0):
                    s, b = (pos[0] // BLK) % SLOTS, pos[0] % BLK
                    if b == 0:
                        tile = pos[0] // BLK
                        e.wait_ge(lo_ready, (tile + 1) if i is None else stride * i + (tile + 1))
                        self.fresh = True
                    pos[0] += 1
                    return whi[:, s, b * P:(b + 1) * P], wlo[:, s, b * P:(b + 1) * P]

                def at_tile_start(self, mm):
                    if self.fresh:
                        mm.then_inc(slots_free, 1)
                        self.fresh = False

                def tile(self):
                    s = (pos[0] // BLK) % SLOTS
                    for _ in range(BLK):
                        self.block()
                    return s

                def skip(self, n):
                    pos[0] += n
            return Reader()

        def product(e, w, out, rh, rl, first, last, i=None, stride=0):
            wh, wl = w.block(i, stride)
            mm = e.matmul(out, wh, rh, start=first, stop=False)
            w.at_tile_start(mm)
            e.matmul(out, wh, rl, start=False, stop=False)
            return e.matmul(out, wl, rh, start=False, stop=last)

        def linear_pe(e, w, f, rh, rl, kb, mt, body, source=None, banks=4):
            iters = mt // body

            def tiles_of(i):
                for m in range(body):
                    e.wait_ge(f.free, (m + 1) if i is None else body * i + (m + 1))
                    for k in range(kb):
                        if source is not None and m == 0:
                            e.wait_ge(source.lo, source.split0 + k + 1)
                        mm = product(e, w, bank[m % banks][:, :], rh[:, k, :], rl[:, k, :],
                                     k == 0, k == kb - 1, i, body * kb // BLK)
                    mm.then_inc(f.full, 1)

            if iters == 1:
                tiles_of(None)
            else:
                with e.Fori(0, iters) as i:
                    tiles_of(i)
                w.skip((iters - 1) * body * kb)

        def looped(e, mt, body, step):
            with e.Fori(0, mt // body) as i:
                for m in range(body):
                    step(body * i + m, m)

        norms = {
            "hgrn": Norm(tiles(h, 8), gains("hgrn_norm", 8), tiles(xh, 8), tiles(xl, 8)),
            "mlp0": Norm(tiles(h, 8), gains("mlp_norm0", 8), tiles(xh, 8), tiles(xl, 8), summed=True),
            "kv": Norm(tiles(h, 8), gains("kv_in_norm", 8), tiles(xh, 8), tiles(xl, 8), summed=True),
            "ckv": Norm(tiles(ckv, 2), gains("kv_norm", 2), tiles(ckh, 2), tiles(ckl, 2), rstd=rstd2),
            "mla": Norm(tiles(h, 8), gains("mla_norm", 8), tiles(xh, 8), tiles(xl, 8), known=True),
            "cq": Norm(tiles(cq, 2), gains("q_norm", 2), tiles(cqh, 2), tiles(cql, 2)),
            "mlp1": Norm(tiles(h, 8), gains("mlp_norm1", 8), tiles(xh, 8), tiles(xl, 8), summed=True),
            "final": Norm(tiles(h, 8), gains("final_norm", 8), o32=tiles(h, 8), summed=True),
            "mix": Norm(tiles(h, 8), gains("norm_mix", 8), tiles(xh, 8), tiles(xl, 8)),
            "c2": Norm([dcraw[:, :]], gains("kv_norm2", 1), o32=[dc[:, :]]),
        }
        split_mo = Split("s_mo", tiles(mo, 16), tiles(moh, 16), tiles(mol, 16))
        split_att = Split("s_att", tiles(dq2, 8), tiles(ath, 8), tiles(atl, 8))
        split_y = Split("s_y", tiles(xs, 16), tiles(yh, 16), tiles(yl, 16))
        split_mg = Split("s_mg", tiles(mg, 8), tiles(xh, 8), tiles(xl, 8))
        norms["ffn"] = Norm(tiles(h, 8), gains("norm_ffn", 8), tiles(xh, 8), tiles(xl, 8), summed=True)
        norms["last"] = Norm(tiles(h, 8), gains("norm_final", 8), o32=tiles(h, 8), summed=True)
        split_og = Split("s_og", tiles(hk, 8), tiles(xh, 8), tiles(xl, 8))
        v_full = sem("v_full")
        lvl_diff, lvl_exp = sem("lvl_diff"), sem("lvl_exp")
        lvl_x, lvl_mm = sem("lvl_x"), sem("lvl_mm")
        st_pe, st_dve = sem("state_pe"), sem("state_dve")
        og_sq, og_sum, og_r = sem("og_sq"), sem("og_sum"), sem("og_r")
        og_t, og_hi = sem("og_t"), sem("og_hi")
        at_s, at_m, at_e = sem("scores_full"), sem("neg_max_ready"), sem("exp_done")
        at_p, at_t, at_c = sem("probs_ready"), sem("probs_t_full"), sem("probs_t_copied")
        at_o, at_oc = sem("attn_out_full"), sem("attn_out_copied")
        ix_full, ix_relu, ix_used = sem("idx_full"), sem("idx_relu"), sem("idx_used")
        flip_full = sem("flip_full")
        y_sum, y_rstd = sem("y_sum"), sem("y_rstd")
        sg_sel, sg_sub, sg_exp = sem("ssm_rows_full"), sem("ssm_diff"), sem("ssm_exp")
        sg_g, sg_y, sg_yd = sem("ssm_g_ready"), sem("ssm_y_full"), sem("ssm_y_done")

        def chunk(c):
            return slice(c * P, (c + 1) * P)

        def four(x):
            return x.rearrange("p (c t) -> p c t", c=ST)

        def to_four(x):
            return x.unsqueeze(1).broadcast_to([P, ST, P])

        def heads_out(x, n):
            return x.unsqueeze(2).broadcast_to([P, n, 64])

        mla = dict(p=pr, pt=pt, mx=mx, nm=nm, rs=rs, ri=ri, scale=MLA_SCALE, first=0)
        dsa = dict(p=pr2, pt=pt2, mx=mx2, nm=nm2, rs=rs2, ri=ri2, scale=1.0, first=64)
        ITEMS = 16

        def attention_pe(e, a, g, scores, value):
            n0 = a["first"] + ITEMS * g
            h0 = n0 // 4

            def out_product(hh):
                e.wait_ge(at_c, n0 + 4 * hh + 4)
                if hh >= 2:
                    e.wait_ge(at_oc, h0 + hh - 1)
                for k in range(ST):
                    mm = e.matmul(bank[5 + hh % 2][:, k * P:], value(hh, k), a["pt"][:, k, k * P:],
                                  start=k == 0, stop=k == ST - 1)
                mm.then_inc(at_o, 1)

            for n in range(ITEMS + 2):
                if n < ITEMS:
                    if n >= 3:
                        e.wait_ge(at_e, n0 + n - 2)
                    scores(n // 4, n % 4, bank[n % 3]).then_inc(at_s, 1)
                m = n - 2
                if m >= 4 and m % 4 == 0:
                    out_product(m // 4 - 1)
                if m >= 0:
                    e.wait_ge(at_p, n0 + m + 1)
                    if m >= 2:
                        e.wait_ge(at_c, n0 + m - 1)
                    for k in range(m % 4 + 1):
                        mm = e.transpose(bank[3 + m % 2][:, chunk(k)], a["p"][:, m % 3, chunk(k)], ident)
                    mm.then_inc(at_t, 1)
            out_product(3)

        def attention_act(e, a, g, logits):
            n0 = a["first"] + ITEMS * g
            h0 = n0 // 4
            for n in range(ITEMS + 2):
                if n < ITEMS:
                    w = (n % 4 + 1) * P
                    q = (n0 + n) % 64
                    e.wait_ge(at_m, n0 + n + 1)
                    if n >= 3:
                        e.wait_ge(at_t, n0 + n - 2)
                    e.activation(a["p"][:, n % 3, 0:w], logits(n)[:, 0:w], ACT.Exp, scale=a["scale"],
                                 bias=a["nm"][:, q:q + 1],
                                 accum_out=a["rs"][:, q:q + 1]).then_inc(at_e, 1)
                m = n - 2
                if m >= 0:
                    i = m % 4
                    e.wait_ge(at_t, n0 + m + 1)
                    if i == 0 and m >= 4:
                        e.wait_ge(at_o, h0 + m // 4)
                    e.activation(a["pt"][:, 0:i + 1, chunk(i)],
                                 bank[3 + m % 2][:, 0:(i + 1) * P].rearrange("p (k q) -> p k q", q=P),
                                 ACT.Copy).then_inc(at_c, 1)

        def attention_dve(e, a, g, logits, out):
            n0 = a["first"] + ITEMS * g
            h0 = n0 // 4

            def copy_out(hh):
                e.wait_ge(at_o, h0 + hh + 1)
                e.tensor_copy(out(hh), bank[5 + hh % 2][:, :]).then_inc(at_oc, 1)

            for n in range(ITEMS + 1):
                if n < ITEMS:
                    w = (n % 4 + 1) * P
                    q = (n0 + n) % 64
                    e.wait_ge(at_s, n0 + n + 1)
                    src = logits(e, n)
                    e.reduce_max(a["mx"][:, q:q + 1], src[:, 0:w], axis=AX.X)
                    e.drain()
                    e.tensor_scalar(a["nm"][:, q:q + 1], a["mx"][:, q:q + 1], -a["scale"], None,
                                    ALU.mult).then_inc(at_m, 1)
                m = n - 1
                if m >= 0:
                    w = (m % 4 + 1) * P
                    q = (n0 + m) % 64
                    e.wait_ge(at_e, n0 + m + 1)
                    e.reciprocal(a["ri"][:, q:q + 1], a["rs"][:, q:q + 1])
                    e.drain()
                    e.tensor_scalar(a["p"][:, m % 3, 0:w], a["p"][:, m % 3, 0:w], a["ri"][:, q:q + 1],
                                    None, ALU.mult).then_inc(at_p, 1)
                if n >= 7 and (n - 7) % 4 == 0:
                    copy_out((n - 7) // 4)
            copy_out(3)

        def half(x, L, part):
            return x[:, 4 * part:4 * part + 4, :].rearrange("p h (n u l) -> p (h n) u l", u=2, l=L)

        @block.tensor
        def _(e):
            join = joiner(e, pe_step, (act_step, dve_step))
            w = weight_reader(e)
            e.drain().then_inc(slots_free, LOOK)
            e.wait_ge(consts_loaded, 32)

            def norm(name):
                norm_pe(e, norms[name])
                join()

            def lin(name, rh, rl, kb, mt, body, source=None):
                linear_pe(e, w, flow[name], rh, rl, kb, mt, body, source)
                join()

            def norm_lin(norm_name, name, mt, body):
                norm_pe(e, norms[norm_name])
                linear_pe(e, w, flow[name], xh, xl, 8, mt, body, norms[norm_name])
                join()

            join()
            join()
            norm_lin("hgrn", "hgrn_q", 8, 4)
            lin("hgrn_f", xh, xl, 8, 8, 4)
            lin("hgrn_g", xh, xl, 8, 8, 4)
            for k in range(8):
                s = w.tile()
                wh, wl = whi[:, s, :], wlo[:, s, :]
                for t in range(ST):
                    for n in range(2):
                        o = bank[2 * t + n][:, :]
                        mm = e.matmul(o, xh[:, k, chunk(t)], wh[:, n * 512:(n + 1) * 512], start=k == 0, stop=False)
                        w.at_tile_start(mm)
                        e.matmul(o, xl[:, k, chunk(t)], wh[:, n * 512:(n + 1) * 512], start=False, stop=False)
                        mm = e.matmul(o, xh[:, k, chunk(t)], wl[:, n * 512:(n + 1) * 512], start=False, stop=k == 7)
            mm.then_inc(v_full, 1)
            join()
            join()
            join()
            join()
            for half_ in range(2):
                for hh in range(4 * half_, 4 * half_ + 4):
                    for c in range(ST):
                        mm = e.matmul(bank[hh][:, chunk(c)], hk[:, hh, chunk(c)], hq[:, hh, chunk(c)],
                                      start=True, stop=True)
                mm.then_inc(lvl_mm, 1)
            for n in range(len(LEVELS)):
                x = (hx, ht)[n % 2]
                for half_ in range(2):
                    e.wait_ge(lvl_x, 2 * n + half_ + 1)
                    for hh in range(4 * half_, 4 * half_ + 4):
                        for c in range(ST):
                            mm = e.matmul(bank[hh][:, chunk(c)], x[:, hh, chunk(c)], x[:, hh, chunk(c)],
                                          start=True, stop=True)
                    mm.then_inc(lvl_mm, 1)
            join()
            join()
            join()
            join()
            for hh in range(HEADS):
                for c in range(ST):
                    mm = e.transpose(bank[hh][:, chunk(c)], ht[:, hh, chunk(c)], ident)
            join()
            join()
            for g in range(2):
                for c in range(ST):
                    for j in range(4):
                        hh = 4 * g + j
                        e.matmul(bank[j][:, chunk(c)], hv[:, c, chunk(hh)], hs[:, hh, chunk(c)],
                                 start=True, stop=c == 0)
                        state = ht[:, hh // 4, chunk(hh % 4)]
                        if c:
                            e.wait_ge(st_dve, 12 * g + 4 * (c - 1) + j + 1)
                            e.matmul(bank[j][:, chunk(c)], state, hx[:, hh, chunk(c)], start=False, stop=True)
                        if c < ST - 1:
                            e.matmul(bank[4 + j][:, chunk(c)], hb[:, hh, chunk(c)], hv[:, c, chunk(hh)],
                                     start=True, stop=True).then_inc(st_pe, 1)
                join()
                join()
            join()
            for hh in range(HEADS):
                e.matmul(bank[hh][:, :], ones, hx[:, hh, :], start=True, stop=True).then_inc(og_sum, 1)
            join()
            join()
            lin("hgrn_o", xh, xl, 8, 8, 4, split_og)

            def mlp(n):
                for k in range(2):
                    if k == 0:
                        norm_lin(f"mlp{n}", f"mlp{n}_up0", 16, 4)
                    else:
                        lin(f"mlp{n}_up1", xh, xl, 8, 16, 4)
                    lin(f"mlp{n}_down{k}", uh, ul, 16, 8, 4)

            mlp(0)
            norm_lin("kv", "kv", 4, 4)
            norm("ckv")
            norm_lin("mla", "dq", 2, 2)
            norm("cq")
            for g in range(4):
                for j in range(4):
                    for k in range(2):
                        product(e, w, bank[j][:, :], ckh[:, k, :], ckl[:, k, :], k == 0, k == 1)
                for j in range(4):
                    for k in range(2):
                        product(e, w, bank[4 + j][:, :], cqh[:, k, :], cql[:, k, :], k == 0, k == 1)
                join()
                join()
                for j in range(4):
                    for k in range(2):
                        product(e, w, bank[j][:, :], cqh[:, k, :], cql[:, k, :], k == 0, k == 1)
                s = w.tile()
                for k in range(2):
                    off = 512 * k
                    for t in range(ST):
                        o = bank[4 + t][:, :]
                        mm = e.matmul(o, ckh[:, k, chunk(t)], whi[:, s, off:off + 512], start=k == 0, stop=False)
                        w.at_tile_start(mm)
                        e.matmul(o, ckl[:, k, chunk(t)], whi[:, s, off:off + 512], start=False, stop=False)
                        e.matmul(o, ckh[:, k, chunk(t)], wlo[:, s, off:off + 512], start=False, stop=k == 1)
                join()
                join()

                def scores(j, i, b):
                    n = (i + 1) * P
                    r = slice(64 * (j % 2), 64 * (j % 2) + 64)
                    e.matmul(b[:, 0:n], gq[:, j, chunk(i)], gk[:, j, 0:n], start=True, stop=False)
                    e.matmul(b[:, 0:n], gr[r, j // 2, chunk(i)], kr[r, 0:n], start=False, stop=False)
                    return e.matmul(b[:, chunk(i)], identr[:, :], negr[:, :], start=False, stop=True)

                attention_pe(e, mla, g, scores, lambda j, k: gv[:, k, chunk(j)])
                join()
            lin("mla_o", moh, mol, 16, 8, 4, split_mo)
            mlp(1)
            norm("final")
            norm_lin("mix", "dsa_in", 6, 6)
            lin("dsa_q", xh, xl, 8, 8, 4)
            norm("c2")
            for c in range(ST):
                e.transpose(bank[0][:, chunk(c)], dsmall[:, chunk(c)], ident)
                e.transpose(bank[1][:, chunk(c)], dc[:, chunk(c)], ident)
            e.wait_ge(extra_loaded, 16 * 5)
            e.matmul(bank[2][0:AHEADS, 0:DISTS], rb[:, :], boh[:, :], start=True, stop=True)
            join()
            join()
            for i in range(1, ST):
                for j in range(8):
                    n = 8 * (i - 1) + j
                    r = slice(64 * (j % 2), 64 * (j % 2) + 64)
                    if n >= 4:
                        e.wait_ge(ix_relu, n - 3)
                    e.matmul(bank[n % 4][:, 0:(i + 1) * P], dqi[r, j // 2, chunk(i)], dki[r, 0:(i + 1) * P],
                             start=True, stop=True).then_inc(ix_full, 1)
            e.wait_ge(ix_relu, 24)
            e.wait_ge(toep_loaded, 16)
            for b in range(8):
                mm = e.matmul(bank[b][:, :], col("flip", 0, P),
                              tp[:, 2 * b:2 * b + 2, :].rearrange("p h j -> p (h j)"), start=True, stop=True)
            mm.then_inc(flip_full, 1)
            join()
            for g in range(4):
                for j in range(4):
                    hh = 4 * g + j
                    r = slice(64 * (hh % 2), 64 * (hh % 2) + 64)
                    e.matmul(bank[j][:, :], wuk[r, hh // 2, :], dq2[r, hh // 2, :], start=True, stop=True)
                join()
                join()

                def scores(j, i, b):
                    n = (i + 1) * P
                    near = b[:, max(i - 1, 0) * P:n]
                    t = slice(P if i == 0 else 0, 2 * P)
                    e.matmul(b[:, 0:n], dql[:, j, chunk(i)], dc[:, 0:n], start=True, stop=False)
                    e.matmul(b[:, 0:n], identr[:, :], dsm[:, i, 0:n], start=False, stop=False)
                    e.matmul(near, identr[:, :], tgh[:, j, t], start=False, stop=False)
                    return e.matmul(near, identr[:, :], tgl[:, j, t], start=False, stop=True)

                attention_pe(e, dsa, g, scores, lambda j, k: dcn[:, k, :])
                join()
                for j in range(4):
                    e.matmul(bank[j // 2][64 * (j % 2):64 * (j % 2) + 64, :], wuv[:, 4 * g + j, :],
                             dlo[:, j, :], start=True, stop=True)
                join()
                join()
            lin("att_out", ath, atl, 8, 8, 4, split_att)
            lin("g_att", xh, xl, 8, 8, 4)
            lin("xbc", xh, xl, 8, 24, 4)
            join()
            join()
            join()
            for c in range(ST):
                e.matmul(bank[0][:, c * 32:(c + 1) * 32], col("tri", 0, P), sad[:, c, :], start=True, stop=True)
                e.matmul(bank[1][:, c * 32:(c + 1) * 32], ones, sad[:, c, :], start=True, stop=True)
                e.matmul(bank[2][0:32, chunk(c)], sad[:, c, :], col("tri", 0, P), start=True, stop=True)
            join()
            join()
            join()
            for g in range(4):
                for c in range(ST):
                    for t in range(4):
                        e.transpose(bank[c][:, chunk(t)], xbc[:, 4 * g + t, chunk(c)], ident)
                    e.transpose(bank[4][:, chunk(c)], xbc[:, 16 + g, chunk(c)], ident)
                    e.matmul(bank[5][:, chunk(c)], xbc[:, 16 + g, chunk(c)], xbc[:, 20 + g, chunk(c)],
                             start=True, stop=True)
                join()
                join()
                for c in range(ST - 1):
                    e.wait_ge(st_dve, 24 + 3 * g + c + 1)
                    e.matmul(bank[c][:, :], sbn[:, c, :], sxd[:, :], start=True, stop=True).then_inc(st_pe, 1)
                join()

                def rows(p):
                    if p >= 2:
                        e.wait_ge(sg_exp, 3 * (4 * g + p - 1))
                    hh = 8 * g + 2 * p
                    for q in range(2):
                        sel = identr[0:32, hh + q:hh + q + 1].broadcast_to([32, P])
                        o = bank[2 * (p % 2) + q][:, :]
                        e.matmul(o, sel, sah[:, :], start=True, stop=False)
                        mm = e.matmul(o, sel, sal[:, :], start=False, stop=True)
                    mm.then_inc(sg_sel, 1)

                rows(0)
                rows(1)
                for p in range(4):
                    n = 4 * g + p
                    if p >= 2:
                        e.wait_ge(sg_yd, n - 1)
                    e.wait_ge(sg_g, n + 1)
                    own, past = bank[4 + 2 * (p % 2)], bank[5 + 2 * (p % 2)]
                    for q in range(2):
                        o = slice(64 * q, 64 * q + 64)
                        for c in range(ST):
                            e.matmul(own[o, chunk(c)], sxn[:, c, 128 * p + 64 * q:128 * p + 64 * q + 64],
                                     sgt[p % 2][q][:, chunk(c)], start=True, stop=True)
                    for c in range(1, ST):
                        mm = e.matmul(past[:, chunk(c)], sst[:, c - 1, chunk(p)],
                                      xbc[:, 20 + g, chunk(c)], start=True, stop=True)
                    mm.then_inc(sg_y, 1)
                    if p < 2:
                        rows(p + 2)
                join()
            lin("z", xh, xl, 8, 16, 4)
            for g in range(4):
                mm = e.matmul(bank[4 + g][:, :], ones, zsum[:, g, :], start=True, stop=True)
            mm.then_inc(y_sum, 1)
            lin("g_ssm", xh, xl, 8, 8, 4)
            lin("ssm_out", yh, yl, 16, 8, 4, split_y)
            lin("w_out", xh, xl, 8, 8, 4, split_mg)
            norm_lin("ffn", "ffn_up", 44, 4)
            lin("ffn_down", fh, fl, FT, 8, 8)
            norm("last")

        @block.scalar
        def _(e):
            join = joiner(e, act_step, (pe_step, dve_step))
            e.wait_ge(consts_loaded, 32)

            def norm(name, alone=True):
                norm_act(e, norms[name])
                if alone:
                    join()

            def gate(name, mt, dst):
                f = flow[name]

                def step(m, j):
                    e.wait_ge(f.full, m + 1)
                    e.wait_ge(f.free, m + 1)
                    e.activation(dst[:, j, :], bank[j][:, :], ACT.Sigmoid).then_inc(f.a, 1)
                looped(e, mt, 4, step)
                join()

            def squares(name):
                f = flow[name]

                def step(m, j):
                    e.wait_ge(f.free, m + 5)
                    e.activation(hsq[:, j, :], h[:, m, :], ACT.Square).then_inc(f.a, 1)
                looped(e, 8, 4, step)
                join()

            def copies(name, outs, scale=1.0):
                f = flow[name]
                for m, places in enumerate(outs):
                    e.wait_ge(f.full, m + 1)
                    for k, (rows, dst) in enumerate(places):
                        mm = e.activation(dst, bank[m % 4][rows, :], ACT.Copy, scale=scale)
                    mm.then_inc(f.free, 1)
                join()

            def whole(dst):
                return [(slice(0, P), dst)]

            e.activation(identr[:, :], ident, ACT.Copy)
            e.activation(negr[:, :], col("neg", 0, P), ACT.Copy)
            join()
            e.activation(lbt[:, 0:2, :], lbt[:, 0:2, :], ACT.Exp)
            join()
            norm("hgrn", False)
            gate("hgrn_q", 8, htmp)
            gate("hgrn_f", 8, htmp)
            gate("hgrn_g", 8, htmp)
            e.wait_ge(v_full, 1)
            join()
            for b in range(4):
                e.activation(hv[:, b // 2, (b % 2) * 512:(b % 2 + 1) * 512], bank[b][:, :], ACT.Copy)
            join()
            e.activation(hb[:, :, :], hb[:, :, :], ACT.Ln)
            join()
            join()
            for n in range(len(LEVELS)):
                x = (hx, ht)[n % 2]
                for half_ in range(2):
                    x4 = x[:, 4 * half_:4 * half_ + 4, :]
                    e.wait_ge(lvl_diff, 2 * n + half_ + 1)
                    e.activation(x4, x4, ACT.Exp).then_inc(lvl_exp, 1)
            join()
            e.activation(hx[:, :, :], hb[:, :, :], ACT.Exp)
            e.activation(ebl[:, :], hb[:, :, :].rearrange("p h (c t) -> p (h c) t", c=ST)[:, :, P - 1],
                         ACT.Exp)
            join()
            e.activation(ht[:, :, :], ht[:, :, :], ACT.Exp)
            join()
            join()
            join()
            for hh in range(HEADS):
                e.activation(hb[:, hh, :], bank[hh][:, :], ACT.Copy)
            join()
            for g in range(2):
                join()
                for j in range(4):
                    e.activation(hk[:, 4 * g + j, :], bank[j][:, :], ACT.Copy)
                join()
            e.activation(hx[:, :, :], hk[:, :, :], ACT.Square)
            join()
            for hh in range(HEADS):
                e.wait_ge(og_sum, hh + 1)
                e.activation(hq[:, hh, :], bank[hh][:, :], ACT.Ln, scale=1.0 / P, bias=col("eps"))
            e.drain()
            e.activation(hq[:, :, :], hq[:, :, :], ACT.Exp, scale=-0.5)
            join()
            join()
            split_act(e, split_og)
            squares("hgrn_o")

            def mlp(n):
                norm(f"mlp{n}", False)
                for k in range(2):
                    f = flow[f"mlp{n}_up{k}"]

                    def step(m, j):
                        e.wait_ge(f.full, m + 1)
                        e.wait_ge(f.b, m + 1)
                        e.activation(ur[:, j, :], bank[j][:, :], ACT.Relu).then_inc(f.free, 1)
                        e.drain()
                        e.activation(uh[:, m, :], ur[:, j, :], ACT.Square).then_inc(f.a, 1)
                    looped(e, 16, 4, step)
                    join()
                    if k:
                        squares(f"mlp{n}_down1")
                    else:
                        join()

            mlp(0)
            e.dma_start(rp[:, :, :], rope).then_inc(extra_loaded, 16)
            norm("kv", False)
            copies("kv", [whole(ckv[:, 0, :]), whole(ckv[:, 1, :]), whole(rt[:, 2, :]), whole(rt[:, 3, :])])
            norm("ckv")
            norm("mla", False)
            copies("dq", [whole(cq[:, 0, :]), whole(cq[:, 1, :])])
            norm("cq")
            for g in range(4):
                join()
                for j in range(4):
                    e.activation(gk[:, j, :], bank[j][:, :], ACT.Copy)
                join()
                join()
                for t in range(ST):
                    e.activation(gv[:, t, :], bank[4 + t][:, :], ACT.Copy)
                join()
                attention_act(e, mla, g, lambda n: bank[n % 3])
                join()
            split_act(e, split_mo)
            squares("mla_o")
            mlp(1)
            norm("final")
            norm("mix", False)
            copies("dsa_in", [
                [(slice(0, P), dsmall[:, :]), (slice(0, 64), dki[0:64, :]), (slice(0, 64), dki[64:P, :])],
                *[whole(dqi[:, j, :]) for j in range(4)], whole(dcraw[:, :])])
            f = flow["dsa_q"]

            def step(m, j):
                e.wait_ge(f.full, m + 1)
                e.activation(dq2[:, m, :], bank[j][:, :], ACT.Copy, scale=0.125).then_inc(f.free, 1)
            looped(e, 8, 4, step)
            join()
            for dst, src in ((boh, bucket), (rb, rel_bias), (wuk, w_uk2), (wuv, w_uv2)):
                e.dma_start(dst[:], src).then_inc(extra_loaded, 16)
            norm("c2")
            join()
            e.activation(dnat[:, :, :], four(bank[0][:, :]), ACT.Copy)
            e.activation(dcn[:, :, :], four(bank[1][:, :]), ACT.Copy)
            e.activation(drow[:, :], bank[2][0:AHEADS, 0:DISTS], ACT.Copy)
            join()
            e.dma_start(toep_dram, drow[:, :]).then_inc(toep_stored, 16)
            e.wait_ge(toep_stored, 16)
            e.dma_start(tp[:, :, :], bass.AP(tensor=toep_dram.tensor, offset=0,
                                             ap=[[1, P], [DISTS, AHEADS], [1, 2 * P]])
                        ).then_inc(toep_loaded, 16)
            for n in range(24):
                e.wait_ge(ix_full, n + 1)
                if n >= 4:
                    e.wait_ge(ix_used, n - 3)
                wd = (n // 8 + 2) * P
                e.activation(dre[:, n % 4, 0:wd], bank[n % 4][:, 0:wd], ACT.Relu).then_inc(ix_relu, 1)
            e.wait_ge(flip_full, 1)
            for b in range(8):
                e.activation(tp[:, 2 * b:2 * b + 2, :].rearrange("p h j -> p (h j)"), bank[b][:, :], ACT.Copy)
            join()
            for g in range(4):
                e.activation(tgh[:, :, :], tp[:, 4 * g:4 * g + 4, :], ACT.Copy)
                join()
                for j in range(4):
                    e.activation(dql[:, j, :], bank[j][:, :], ACT.Copy)
                join()
                attention_act(e, dsa, g, lambda n: bank[n % 3])
                join()
                join()
                for j in range(2):
                    e.activation(dq2[:, 2 * g + j, :], bank[j][:, :], ACT.Copy)
                join()
            split_act(e, split_att)
            f = flow["att_out"]

            def step_att(m, j):
                e.wait_ge(f.full, m + 1)
                e.activation(mg[:, m, :], bank[j][:, :], ACT.Copy).then_inc(f.free, 1)
            looped(e, 8, 4, step_att)
            join()
            gate("g_att", 8, gsig)

            fx = flow["xbc"]

            def step_conv(m, j):
                e.wait_ge(fx.full, m + 1)
                e.wait_ge(fx.b, m + 1)
                e.activation(cu[:, j % 2, 3:3 + S], bank[j][:, :], ACT.Copy).then_inc(fx.free, 1)
                e.wait_ge(fx.b, m + 3)
                e.activation(cs[:, j % 2, :], ca[:, j, :], ACT.Sigmoid).then_inc(fx.a, 1)
            looped(e, 24, 4, step_conv)
            join()
            join()
            e.activation(sz[:, 2, :], sz[:, 1, :], ACT.Exp)
            e.activation(sam[:, :], col("a_log", 0, 32), ACT.Exp)
            join()
            join()
            join()
            e.activation(sah[:, :], bank[2][0:32, :], ACT.Copy)
            join()
            e.activation(scd[:, :, :], sat[:, :, :], ACT.Exp)
            e.activation(sds[:, :, :], sds[:, :, :], ACT.Exp)
            join()
            for g in range(4):
                join()
                e.activation(sbn[:, :, :], four(bank[4][:, :]), ACT.Copy)
                join()
                join()
                for p in range(4):
                    n = 4 * g + p
                    for q in range(2):
                        e.wait_ge(sg_sub, 2 * n + q + 1)
                        x = sgt[p % 2][q]
                        e.activation(x[:, :], x[:, :], ACT.Exp).then_inc(sg_exp, 1)
                    if p >= 2:
                        e.wait_ge(sg_yd, n - 1)
                    for q in range(2):
                        o = slice(64 * q, 64 * q + 64)
                        mm = e.activation(sea[p % 2][o, :], bank[2 * (p % 2) + q][o, :], ACT.Exp)
                    mm.then_inc(sg_exp, 1)
                join()
            fz = flow["z"]

            def step_z(m, j):
                e.wait_ge(fz.a, 2 * m + 1)
                e.activation(zsq[:, j, :], zt[:, j, :], ACT.Sigmoid).then_inc(fz.b, 1)
                e.wait_ge(fz.a, 2 * m + 2)
                e.activation(zsq[:, j, :], xbc[:, m, :], ACT.Square).then_inc(fz.b, 1)
            looped(e, 16, 4, step_z)
            join()
            e.wait_ge(y_sum, 1)
            for g in range(4):
                e.activation(grs[:, g, :], bank[4 + g][:, :], ACT.Ln, scale=1.0 / 512, bias=col("eps"))
            e.drain()
            e.activation(grs[:, :, :], grs[:, :, :], ACT.Exp, scale=-0.5).then_inc(y_rstd, 1)
            f2 = flow["g_ssm"]

            def step_gss(m, j):
                e.wait_ge(f2.full, m + 1)
                e.activation(gss[:, m, :], bank[j][:, :], ACT.Sigmoid).then_inc(f2.free, 1)
            looped(e, 8, 4, step_gss)
            join()
            split_act(e, split_y)
            join()
            split_act(e, split_mg)
            squares("w_out")
            norm("ffn", False)
            ff = flow["ffn_up"]

            with e.Fori(0, FT // 2) as i:
                for r in range(2):
                    m, pair = 4 * i + 2 * r, 2 * i + r
                    for k in range(2):
                        e.wait_ge(ff.full, m + (k + 1))
                        e.wait_ge(ff.b, m + (k + 1))
                        e.activation(fu[:, 2:2 + S], bank[2 * r + k][:, :], ACT.Copy).then_inc(ff.free, 1)
                    e.activation(fs[:, :], fa[:, :], ACT.Sigmoid).then_inc(ff.a, 1)
                    e.wait_ge(ff.c, pair + 1)
                    e.activation(fh[:, pair, :], fa[:, :], ACT.Copy).then_inc(ff.a, 1)
            join()
            squares("ffn_down")
            norm("last")
            e.dma_start(out, h[:, :, :]).then_inc(stored, 16)
            e.wait_ge(stored, 16)

        @block.vector
        def _(e):
            join = joiner(e, dve_step, (pe_step, act_step))
            tt, ts, stt = e.tensor_tensor, e.tensor_scalar, e.scalar_tensor_tensor
            for f in flow.values():
                e.drain().then_inc(f.free, 4)
            e.wait_ge(consts_loaded, 32)

            def norm(name, alone=True):
                norm_dve(e, norms[name])
                if alone:
                    join()

            def gated(name, mt, put):
                f = flow[name]

                def step(m, j):
                    e.wait_ge(f.a, m + 1)
                    put(m, j).then_inc(f.free, 1)
                looped(e, mt, 4, step)
                join()

            def residual(name, sums=True):
                f = flow[name]
                if sums:
                    e.drain()
                    e.memset(sqsum[:, :], 0.0)

                def step(m, j):
                    e.wait_ge(f.full, m + 1)
                    tt(h[:, m, :], bank[j][:, :], h[:, m, :], ALU.add).then_inc(f.free, 1)
                    if sums:
                        e.drain()
                        e.wait_ge(f.a, m + 1)
                        tt(sqsum[:, :], sqsum[:, :], hsq[:, j, :], ALU.add)
                looped(e, 8, 4, step)
                join()

            tt(lbt[:, 2, :], col("lb0", 0, 8), col("lb1", 0, 8), ALU.max)
            e.drain()
            tt(lbt[:, 0, :], col("lb0", 0, 8), lbt[:, 2, :], ALU.subtract)
            tt(lbt[:, 1, :], col("lb1", 0, 8), lbt[:, 2, :], ALU.subtract)
            join()
            join()
            tt(lbt[:, 2, :], lbt[:, 0, :], lbt[:, 1, :], ALU.add)
            e.drain()
            e.reciprocal(lbt[:, 1, :], lbt[:, 2, :])
            e.drain()
            tt(lb[:, :], lbt[:, 0, :], lbt[:, 1, :], ALU.mult)
            e.drain()
            ts(oml[:, :], lb[:, :], -1.0, 1.0, ALU.mult, ALU.add)
            norm("hgrn", False)
            gated("hgrn_q", 8, lambda m, j: tt(hq[:, m, :], bank[j][:, :], htmp[:, j, :], ALU.mult))
            gated("hgrn_f", 8, lambda m, j: ts(hb[:, m, :], htmp[:, j, :], oml[:, bass.ds(m, 1)],
                                               lb[:, bass.ds(m, 1)], ALU.mult, ALU.add))
            gated("hgrn_g", 8, lambda m, j: tt(hg[:, m, :], bank[j][:, :], htmp[:, j, :], ALU.mult))
            e.wait_ge(v_full, 1)
            join()
            for b in range(4, 8):
                e.tensor_copy(hv[:, b // 2, (b % 2) * 512:(b % 2 + 1) * 512], bank[b][:, :])
            ts(hk[:, :, :], hb[:, :, :], -1.0, 1.0, ALU.mult, ALU.add)
            join()
            join()
            for hh in range(HEADS):
                e.tensor_tensor_scan(hb[:, hh, :], col("restart", 0, S), hb[:, hh, :], 0.0, ALU.mult, ALU.add)
            join()

            def level_exponents(n, part):
                L = LEVELS[n]
                x, b = half((hx, ht)[n % 2], L, part), half(hb, L, part)
                mid = b[:, :, 0, L - 1:L].broadcast_to([P, 4 * S // (2 * L), L])
                tt(x[:, :, 1, :], b[:, :, 1, :], mid, ALU.subtract)
                tt(x[:, :, 0, :], mid, b[:, :, 0, :], ALU.subtract).then_inc(lvl_diff, 1)

            def place_level(n, part):
                e.wait_ge(lvl_mm, 2 * n + part + 3)
                e.drain()
                for hh in range(4 * part, 4 * part + 4):
                    e.copy_predicated(four(hs[:, hh, :]), to_four(col("levels", n * P, P).bitcast(I32)),
                                      four(bank[hh][:, :]))

            level_exponents(0, 0)
            level_exponents(0, 1)
            for part in range(2):
                e.wait_ge(lvl_mm, part + 1)
                for hh in range(4 * part, 4 * part + 4):
                    tt(four(hs[:, hh, :]), four(bank[hh][:, :]), to_four(ident), ALU.mult)
            for n in range(len(LEVELS)):
                L = LEVELS[n]
                for part in range(2):
                    if n:
                        place_level(n - 1, part)
                    if n + 1 < len(LEVELS):
                        level_exponents(n + 1, part)
                    e.wait_ge(lvl_exp, 2 * n + part + 1)
                    x = half((hx, ht)[n % 2], L, part)
                    tt(x[:, :, 1, :], x[:, :, 1, :], half(hq, L, part)[:, :, 1, :], ALU.mult)
                    tt(x[:, :, 0, :], x[:, :, 0, :], half(hk, L, part)[:, :, 0, :], ALU.mult).then_inc(lvl_x, 1)
            for part in range(2):
                place_level(len(LEVELS) - 1, part)
            join()
            b4 = hb[:, :, :].rearrange("p h (c t) -> p (h c) t", c=ST)
            t4 = ht[:, :, :].rearrange("p h (c t) -> p (h c) t", c=ST)
            tt(t4, b4[:, :, P - 1:P].broadcast_to([P, HEADS * ST, P]), b4, ALU.subtract)
            join()
            tt(hx[:, :, :], hx[:, :, :], hq[:, :, :], ALU.mult)
            join()
            tt(ht[:, :, :], ht[:, :, :], hk[:, :, :], ALU.mult)
            join()
            join()
            join()
            for g in range(2):
                for c in range(ST - 1):
                    for j in range(4):
                        hh = 4 * g + j
                        state, upd = ht[:, hh // 4, chunk(hh % 4)], bank[4 + j][:, chunk(c)]
                        e.wait_ge(st_pe, 12 * g + 4 * c + j + 1)
                        if c == 0:
                            e.tensor_copy(state, upd).then_inc(st_dve, 1)
                        else:
                            stt(state, state, ebl[:, ST * hh + c:ST * hh + c + 1], upd,
                                ALU.mult, ALU.add).then_inc(st_dve, 1)
                join()
                join()
            join()
            join()
            for hh in range(HEADS):
                stt(hk[:, hh, :], hk[:, hh, :], col("g_norm"), hq[:, hh, :], ALU.mult, ALU.mult)
            e.drain()
            tt(hk[:, :, :], hk[:, :, :], hg[:, :, :], ALU.mult)
            join()
            split_dve(e, split_og)
            residual("hgrn_o")

            def mlp(n):
                norm(f"mlp{n}", False)
                for k in range(2):
                    f = flow[f"mlp{n}_up{k}"]
                    e.drain().then_inc(f.b, 4)

                    def step(m, j):
                        e.wait_ge(f.free, m + 5)
                        tt(ut[:, j, :], ur[:, j, :], ur[:, j, :], ALU.mult)
                        e.drain()
                        e.wait_ge(f.a, m + 1)
                        tt(ul[:, m, :], ut[:, j, :], uh[:, m, :].bitcast(F32), ALU.subtract).then_inc(f.b, 1)
                    looped(e, 16, 4, step)
                    join()
                    residual(f"mlp{n}_down{k}", k == 1)

            def rotate(x, swapped, o, t):
                tt(rt[:, t, :], x, rp[:, 0, :], ALU.mult)
                tt(o, swapped, rp[:, 1, :], ALU.mult)
                e.drain()
                tt(o, rt[:, t, :], o, ALU.add)

            mlp(0)
            norm("kv", False)
            join()
            e.wait_ge(extra_loaded, 16)
            rotate(rt[:, 2, :], rt[:, 3, :], kr[:, :], 0)
            norm("ckv")
            norm("mla", False)
            join()
            norm("cq")
            for g in range(4):
                join()
                for j in range(4):
                    e.tensor_copy(gq[:, j, :], bank[4 + j][:, :])
                join()
                join()
                for t in range(2):
                    rotate(bank[t][:, :], bank[2 + t][:, :], gr[:, t, :], t)
                join()
                attention_dve(e, mla, g, lambda e_, n: bank[n % 3], lambda j: mo[:, 4 * g + j, :])
                join()
            split_dve(e, split_mo)
            residual("mla_o")
            mlp(1)
            norm("final")
            norm("mix", False)
            join()
            join()
            norm("c2")
            join()
            join()
            for i in range(1, ST):
                wd = (i + 1) * P
                acc = dsc[:, i - 1, 0:wd]
                for j in range(8):
                    n = 8 * (i - 1) + j
                    wcol = dnat[:, i, 64 + j:65 + j]
                    e.wait_ge(ix_relu, n + 1)
                    if j == 0:
                        ts(acc, dre[:, n % 4, 0:wd], wcol, None, ALU.mult).then_inc(ix_used, 1)
                    else:
                        e.drain()
                        stt(acc, dre[:, n % 4, 0:wd], wcol, acc, ALU.mult, ALU.add).then_inc(ix_used, 1)
                e.drain()
                tt(dsc[:, i - 1, chunk(i)], dsc[:, i - 1, chunk(i)], col("neg", 0, P), ALU.add)
            e.drain()
            for t in range(TOPK // 8):
                for i in range(1, ST):
                    e.max(dm8[:, i - 1, :], (dwk if t else dsc)[:, i - 1, 0:(i + 1) * P])
                e.drain()
                for i in range(1, ST):
                    wd = (i + 1) * P
                    e.match_replace(dwk[:, i - 1, 0:wd], dm8[:, i - 1, :], (dwk if t else dsc)[:, i - 1, 0:wd],
                                    TAKEN)
                e.drain()
            e.tensor_copy(dsm[:, 0, 0:P], col("neg", 0, P))
            for i in range(1, ST):
                wd = (i + 1) * P
                ts(dsm[:, i, 0:wd], dwk[:, i - 1, 0:wd], TAKEN / 2, NEG, ALU.is_ge, ALU.mult)
            join()
            for g in range(4):
                join()
                tt(tgl[:, :, :], tp[:, 4 * g:4 * g + 4, :], tgh[:, :, :].bitcast(F32), ALU.subtract)
                join()
                attention_dve(e, dsa, g, lambda e_, n: bank[n % 3], lambda j: dlo[:, j, :])
                join()
                join()
                join()
            split_dve(e, split_att)
            join()
            gated("g_att", 8, lambda m, j: tt(mg[:, m, :], mg[:, m, :], gsig[:, j, :], ALU.mult))

            def convolve(dst, src, taps, name, nt_, m):
                ts(dst, src[:, 0:S], C[:, bass.ds(COL[name] + m, 1)], C[:, bass.ds(COL[name + "_b"] + m, 1)],
                   ALU.mult, ALU.add)
                for k in range(1, taps):
                    e.drain()
                    last = stt(dst, src[:, k:k + S], C[:, bass.ds(COL[name] + k * nt_ + m, 1)], dst,
                               ALU.mult, ALU.add)
                return last

            fx = flow["xbc"]
            e.memset(cu[:, :, 0:3], 0.0)
            e.drain().then_inc(fx.b, 2)

            def step_conv(m, j):
                e.wait_ge(fx.free, m + 5)
                convolve(ca[:, j, :], cu[:, j % 2, :], 4, "conv_ssm", 24, m).then_inc(fx.b, 1)
                e.wait_ge(fx.a, m + 1)
                tt(xbc[:, m, :], ca[:, j, :], cs[:, j % 2, :], ALU.mult)
            looped(e, 24, 4, step_conv)
            join()

            def z3(k):
                return sz[:, k, :].rearrange("p (c n) -> p c n", n=32)

            tt(z3(0), dnat[:, :, 96:P], col("dt_bias", 0, 32).unsqueeze(1).broadcast_to([P, ST, 32]), ALU.add)
            e.drain()
            stt(sz[:, 1, :], sz[:, 0, :], -1.0, sz[:, 0, :], ALU.mult, ALU.min)
            join()
            join()
            z0, z1, z2, z4, z5 = (sz[:, k, :] for k in (0, 1, 2, 4, 5))
            ts(z1, z2, 2.0, None, ALU.add)
            e.drain()
            e.reciprocal(z5, z1)
            e.drain()
            tt(z4, z2, z5, ALU.mult)
            e.drain()
            tt(z1, z4, z4, ALU.mult)
            e.drain()
            ts(z5, z1, 1.0 / 15, 1.0 / 13, ALU.mult, ALU.add)
            for k in (11, 9, 7, 5, 3, 1):
                e.drain()
                tt(z5, z5, z1, ALU.mult)
                e.drain()
                ts(z5, z5, 1.0 / k, None, ALU.add)
            e.drain()
            tt(z5, z5, z4, ALU.mult)
            e.drain()
            ts(z5, z5, 2.0, None, ALU.mult)
            ts(z0, z0, 0.0, None, ALU.max)
            e.drain()
            tt(sdt[:, :, :], z3(5), z3(0), ALU.add)
            e.drain()
            stt(sad[:, :, :], sdt[:, :, :], -1.0, sam[:, :].unsqueeze(1).broadcast_to([P, ST, 32]),
                ALU.mult, ALU.mult)
            join()
            join()
            e.tensor_copy(sac[:, :, :], bank[0][:, 0:P].rearrange("p (c n) -> p c n", n=32))
            e.tensor_copy(sat[:, :, :], bank[1][:, 0:P].rearrange("p (c n) -> p c n", n=32))
            e.drain()
            tt(sds[:, :, :], sat[:, :, :], sac[:, :, :], ALU.subtract)
            join()
            tt(sal[:, :], bank[2][0:32, :], sah[:, :].bitcast(F32), ALU.subtract)
            join()
            for g in range(4):
                g8 = slice(8 * g, 8 * g + 8)

                def by_head(x):
                    return x.rearrange("p (n d) -> p n d", d=64)

                join()
                for c in range(ST):
                    tt(by_head(sxn[:, c, :]), by_head(bank[c][:, :]), heads_out(sdt[:, c, g8], 8), ALU.mult)
                tt(scb[:, :, :], four(bank[5][:, :]), to_four(col("tri", 0, P)), ALU.mult)
                join()
                for c in range(ST - 1):
                    n = 24 + 3 * g + c
                    if c:
                        e.drain()
                    tt(by_head(sxd[:, :]), by_head(sxn[:, c, :]), heads_out(sds[:, c, g8], 8),
                       ALU.mult).then_inc(st_dve, 1)
                    if c:
                        tt(by_head(sst[:, c, :]), by_head(sst[:, c - 1, :]), heads_out(scd[:, c, g8], 8), ALU.mult)
                        e.drain()
                    e.wait_ge(st_pe, n + 1)
                    if c:
                        tt(sst[:, c, :], sst[:, c, :], bank[c][:, :], ALU.add)
                    else:
                        e.tensor_copy(sst[:, 0, :], bank[0][:, :])
                join()

                def differences(p):
                    n, hh = 4 * g + p, 8 * g + 2 * p
                    if p >= 2:
                        e.wait_ge(sg_y, n - 1)
                    e.wait_ge(sg_sel, n + 1)
                    for q in range(2):
                        tt(four(sgt[p % 2][q][:, :]), four(bank[2 * (p % 2) + q][:, :]),
                           sac[:, :, hh + q:hh + q + 1].broadcast_to([P, ST, P]), ALU.subtract)
                    e.drain()
                    for q in range(2):
                        x = sgt[p % 2][q]
                        ts(x[:, :], x[:, :], 0.0, None, ALU.min).then_inc(sg_sub, 1)

                def take_y(p):
                    n = 4 * g + p
                    x, ea = xbc[:, n, :], sea[p % 2]
                    e.wait_ge(sg_y, n + 1)
                    e.wait_ge(sg_exp, 3 * n + 3)
                    tt(ea[:, P:S], bank[5 + 2 * (p % 2)][:, P:S], ea[:, P:S], ALU.mult)
                    stt(x, x, col("d_skip", n), bank[4 + 2 * (p % 2)][:, :], ALU.mult, ALU.add)
                    e.drain()
                    tt(x[:, P:S], x[:, P:S], ea[:, P:S], ALU.add).then_inc(sg_yd, 1)

                differences(0)
                for p in range(4):
                    if p < 3:
                        differences(p + 1)
                    e.wait_ge(sg_exp, 3 * (4 * g + p) + 2)
                    for q in range(2):
                        x = sgt[p % 2][q]
                        mm = tt(x[:, :], x[:, :], scb[:, :, :].rearrange("p c t -> p (c t)"), ALU.mult)
                    mm.then_inc(sg_g, 1)
                    if p:
                        take_y(p - 1)
                take_y(3)
                join()

            fz = flow["z"]
            e.memset(zsum[:, :, :], 0.0)
            with e.Fori(0, 4) as i:
                for j in range(4):
                    m = 4 * i + j
                    e.wait_ge(fz.full, m + 1)
                    e.tensor_copy(zt[:, j, :], bank[j][:, :]).then_inc(fz.a, 1)
                    e.wait_ge(fz.b, 2 * m + 1)
                    tt(zt[:, j, :], zt[:, j, :], zsq[:, j, :], ALU.mult).then_inc(fz.free, 1)
                    e.drain()
                    tt(xbc[:, m, :], xbc[:, m, :], zt[:, j, :], ALU.mult).then_inc(fz.a, 1)
                    e.wait_ge(fz.b, 2 * m + 2)
                    tt(zsum[:, bass.ds(i, 1), :], zsum[:, bass.ds(i, 1), :], zsq[:, j:j + 1, :], ALU.add)
            join()
            e.wait_ge(y_rstd, 1)
            for t in range(16):
                stt(xbc[:, t, :], xbc[:, t, :], col("ssm_norm", t), grs[:, t // 4, :], ALU.mult, ALU.mult)
            join()
            split_dve(e, split_y)
            fo = flow["ssm_out"]

            def step_out(m, j):
                e.wait_ge(fo.full, m + 1)
                tt(sq[:, j, :], bank[j][:, :], gss[:, m, :], ALU.mult)
                e.drain()
                tt(mg[:, m, :], mg[:, m, :], sq[:, j, :], ALU.add).then_inc(fo.free, 1)
            looped(e, 8, 4, step_out)
            join()
            split_dve(e, split_mg)
            residual("w_out")
            norm("ffn", False)
            ff = flow["ffn_up"]
            e.memset(fu[:, 0:2], 0.0)
            e.drain().then_inc(ff.b, 1)
            with e.Fori(0, FT // 2) as i:
                for r in range(2):
                    m, pair = 4 * i + 2 * r, 2 * i + r
                    e.wait_ge(ff.free, m + 5)
                    convolve(fa[:, :], fu, 3, "conv_ffn", 44, m).then_inc(ff.b, 1)
                    e.wait_ge(ff.free, m + 6)
                    convolve(fv[:, :], fu, 3, "conv_ffn", 44, m + 1).then_inc(ff.b, 1)
                    e.wait_ge(ff.a, 2 * pair + 1)
                    tt(fa[:, :], fa[:, :], fs[:, :], ALU.mult)
                    e.drain()
                    tt(fa[:, :], fa[:, :], fv[:, :], ALU.mult).then_inc(ff.c, 1)
                    e.wait_ge(ff.a, 2 * pair + 2)
                    tt(fl[:, pair, :], fa[:, :], fh[:, pair, :].bitcast(F32), ALU.subtract)
                    e.drain()
            join()
            residual("ffn_down")
            norm("last")


def blocks(w):
    k, m = w.shape[0] // P, w.shape[1] // P
    return w.reshape(k, P, m, P).transpose(2, 0, 1, 3).reshape(k * m, P, P)


def row_blocks(w):
    k, m = w.shape[0] // P, w.shape[1] // P
    return w.reshape(k, P, m, P).transpose(0, 2, 1, 3).reshape(k * m, P, P)


def weight_stream(a):
    out = []
    for n in ("hgrn_w_q", "hgrn_w_f", "hgrn_w_g"):
        out.append(blocks(a[n][0]))
    out += [row_blocks(a["hgrn_w_i"][0]), blocks(a["hgrn_w_o"][0])]

    def mlp(n):
        up, down = a["mlp_w_up"][n], a["mlp_w_down"][n]
        hf = D_FF // 2
        for k in range(2):
            out.extend([blocks(up[:, k * hf:(k + 1) * hf]), blocks(down[k * hf:(k + 1) * hf])])

    mlp(0)
    dkv = a["kv_w_dkv"]
    x1, x2 = dkv[:, 256:288], dkv[:, 288:320]
    out.append(blocks(np.concatenate([dkv[:, :256], x1, x2, x1, x2, x2, x1, x2, x1], 1)))
    out.append(blocks(a["mla_w_dq"][0]))
    uq = a["mla_w_uq"][0].reshape(256, 16, 192)
    uk, uv = a["kv_w_uk"], a["kv_w_uv"]
    for g in range(4):
        hs = slice(4 * g, 4 * g + 4)
        out.append(blocks(uk[:, 512 * g:512 * (g + 1)]))
        out.append(blocks(uq[:, hs, :128].reshape(256, 512)))
        x1, x2 = uq[:, hs, 128:160], uq[:, hs, 160:192]
        out.append(blocks(np.concatenate([np.concatenate([x1, x2], 2).reshape(256, 256),
                                          np.concatenate([x2, x1], 2).reshape(256, 256)], 1)))
        out.append(row_blocks(uv[:, 512 * g:512 * (g + 1)]))
    out.append(blocks(a["mla_w_o"][0]))
    mlp(1)
    w = a["w_in_2"][0]
    q, c, qi, ki, wi, z, xbc, dt, ga, gs = np.split(w, np.cumsum([1024, 128, 512, 64, 8, 2048, 3072, 32, 1024]), 1)
    small = np.concatenate([ki, wi, np.zeros((D, 24), w.dtype), dt], 1)
    out += [blocks(small), blocks(qi), blocks(c), blocks(q), blocks(a["w_att_out_2"][0]), blocks(ga),
            blocks(xbc), blocks(z), blocks(gs), blocks(a["w_ssm_out_2"][0]), blocks(a["w_out_2"][0])]
    up = a["w_ffn_up_2"][0].reshape(D, 2, FT, P).transpose(0, 2, 1, 3).reshape(D, 2 * FFN)
    out += [blocks(up), blocks(a["w_ffn_down_2"][0])]
    s = np.concatenate(out)
    s = np.concatenate([s, np.zeros((TILES * BLK - s.shape[0], P, P), s.dtype)])
    return np.ascontiguousarray(s.reshape(TILES, BLK, P, P).transpose(0, 2, 1, 3)).reshape(TILES, P, BLK * P)


def columns(a):
    c = np.zeros((P, NCOLS), np.float32)

    def put(name, x, rows=P):
        c[:rows, COL[name]:COL[name] + x.shape[1]] = x

    i = np.arange(P)
    put("ident", np.eye(P, dtype=np.float32))
    put("ones", np.ones((P, P), np.float32))
    put("neg", np.where(i[None, :] > i[:, None], NEG, 0.0).astype(np.float32))
    put("tri", (i[:, None] <= i[None, :]).astype(np.float32))
    put("flip", np.ascontiguousarray(np.eye(P, dtype=np.float32)[::-1]))
    put("restart", np.tile((np.arange(S) % P != 0).astype(np.float32), (P, 1)))
    for n, L in enumerate(LEVELS):
        same = i[:, None] // (2 * L) == i[None, :] // (2 * L)
        put_at = COL["levels"] + n * P
        c[:, put_at:put_at + P] = same & (i[:, None] % (2 * L) < L) & (i[None, :] % (2 * L) >= L)
    put("eps", np.full((P, 1), EPS, np.float32))

    def feat(x):
        return x.reshape(-1, P).T

    for name, x in (("hgrn_norm", a["hgrn_norm"][0]), ("mla_norm", a["mla_norm"][0]),
                    ("kv_in_norm", a["kv_in_norm"]), ("mlp_norm0", a["mlp_norm"][0]),
                    ("mlp_norm1", a["mlp_norm"][1]), ("final_norm", a["final_norm"]),
                    ("norm_mix", a["norm_mix_2"][0]), ("norm_ffn", a["norm_ffn_2"][0]),
                    ("norm_final", a["norm_final_2"]), ("g_norm", a["hgrn_g_norm"][0]),
                    ("lb0", a["hgrn_lb_logits"][0]), ("lb1", a["hgrn_lb_logits"][1]),
                    ("q_norm", a["mla_q_norm"][0]), ("kv_norm", a["kv_norm"]),
                    ("kv_norm2", a["kv_norm_2"][0]), ("ssm_norm", a["ssm_norm_2"][0]),
                    ("conv_ssm_b", a["conv_ssm_b_2"][0]),
                    ("d_skip", np.repeat(a["d_skip_2"][0], 64))):
        put(name, feat(x))
    put("dt_bias", np.tile(a["dt_bias_2"][0], (P, 1)))
    put("a_log", np.tile(a["a_log_2"][0], (P, 1)))
    put("conv_ssm", feat(a["conv_ssm_w_2"][0].reshape(-1)))

    def pairs(x):
        return x.reshape(-1, 2, FT, P).transpose(0, 2, 1, 3).reshape(-1)

    put("conv_ffn", feat(pairs(a["conv_ffn_w_2"][0])))
    put("conv_ffn_b", feat(pairs(a["conv_ffn_b_2"][0])))
    return c


def rope_rows():
    f = (np.float32(10000.0) ** (-np.arange(32, dtype=np.float32) / np.float32(32))).astype(np.float32)
    ang = np.arange(S, dtype=np.float32)[None, :] * f[:, None]
    cos, sin = np.cos(ang).astype(np.float32), np.sin(ang).astype(np.float32)
    return np.stack([np.concatenate([cos, cos, cos, cos]), np.concatenate([-sin, sin, -sin, sin])], 1)


def bucket_rows():
    dist = np.maximum(255 - np.arange(DISTS), 0)
    large = 16 + (np.log(np.maximum(dist, 1).astype(np.float32) / np.float32(16)).astype(np.float32)
                  / np.float32(np.log(8.0)) * np.float32(16)).astype(np.int32)
    b = np.where(dist < 16, dist, np.minimum(large, 31))
    one = (np.arange(BUCKETS)[:, None] == b[None, :]).astype(np.float32)
    one[31] -= 1.0
    return one


def kernel(**inputs):
    import concourse.bacc as bacc
    from concourse.bass_utils import run_bass_kernel_spmd

    a = {k: np.asarray(v) for k, v in inputs.items()}
    arrays = {
        "stream": weight_stream(a),
        "cols": columns(a),
        "rope": rope_rows(),
        "bucket": bucket_rows(),
        "w_uk2": np.ascontiguousarray(a["w_uk_2"][0].reshape(8, P, P).transpose(1, 0, 2)),
        "w_uv2": np.ascontiguousarray(a["w_uv_2"][0].transpose(2, 0, 1)),
        "x_in": np.ascontiguousarray(a["x"][0].reshape(S, KT, P).transpose(2, 1, 0)),
        "rel_bias": np.ascontiguousarray(a["rel_bias_2"]),
    }
    nc = bacc.Bacc("TRN2", target_bir_lowering=False, num_devices=1)
    args = [nc.dram_tensor(n, x.shape, F32, kind="ExternalInput").ap() for n, x in arrays.items()]
    toep = nc.dram_tensor("bias_by_distance", (AHEADS, DISTS), F32, kind="Internal").ap()
    out = nc.dram_tensor("out", (P, KT, S), F32, kind="ExternalOutput").ap()
    build(nc, *args, toep, out)
    r = run_bass_kernel_spmd(nc, [arrays], core_ids=[0])
    got = r.results[0]["out"]
    return np.ascontiguousarray(got.transpose(2, 1, 0)).reshape(1, S, D)
```
